# Optimizing a Trainium2 kernel written in Bass

```python
import math
import jax, jax.numpy as jnp
from jax import lax
import numpy as np

D_MODEL = 2048
BATCH = 1
SEQ = 512
DEPTH = 1

MLA_V_DIM = 128
MLA_HEADS = (D_MODEL // 2) // MLA_V_DIM
MLA_NOPE_DIM = 128
MLA_ROPE_DIM = 64
MLA_QK_DIM = MLA_NOPE_DIM + MLA_ROPE_DIM
Q_LORA_RANK = 512
KV_LORA_RANK = 512
ROPE_THETA = 10000.0
SWA_HEAD_DIM = 64
SWA_HEADS = (D_MODEL // 2) // SWA_HEAD_DIM
SWA_KV_HEADS = 2
SWA_GROUP = SWA_HEADS // SWA_KV_HEADS
WINDOW = 128
NUM_BUCKETS = 32
MAX_DISTANCE = 128
Q_BLOCK = 128
MIX_WIDTH = MLA_HEADS * MLA_V_DIM + SWA_HEADS * SWA_HEAD_DIM
D_FF = ((-(-8 * D_MODEL // 3)) + 255) // 256 * 256
IN_SIZES = (Q_LORA_RANK, KV_LORA_RANK, MLA_ROPE_DIM,
            SWA_HEADS * SWA_HEAD_DIM, SWA_KV_HEADS * SWA_HEAD_DIM, SWA_KV_HEADS * SWA_HEAD_DIM)
IN_WIDTH = sum(IN_SIZES)
RMS_EPS = 1e-6
NEG_INF = -1e30

kernel_name = "hymba_mla_swa_sink_t5_sandwich"

def rms_norm(x, g):
    xf = x.astype(jnp.float32)
    y = xf * lax.rsqrt(jnp.mean(xf * xf, axis=-1, keepdims=True) + RMS_EPS)
    return (y * g.astype(jnp.float32)).astype(x.dtype)

def rope(t, positions):
    half = t.shape[-1] // 2
    inv_freq = ROPE_THETA ** (-jnp.arange(half, dtype=jnp.float32) / half)
    ang = positions.astype(jnp.float32)[..., None] * inv_freq
    cos = jnp.cos(ang)[:, :, None, :]
    sin = jnp.sin(ang)[:, :, None, :]
    tf = t.astype(jnp.float32)
    t1, t2 = tf[..., :half], tf[..., half:]
    return jnp.concatenate([t1 * cos - t2 * sin, t2 * cos + t1 * sin], axis=-1).astype(t.dtype)

def t5_causal_bucket(dist):
    max_exact = NUM_BUCKETS // 2
    dist = np.maximum(dist, 0)
    large = max_exact + (np.log(np.maximum(dist, 1) / max_exact)
                         / np.log(MAX_DISTANCE / max_exact)
                         * (NUM_BUCKETS - max_exact)).astype(np.int32)
    large = np.minimum(large, NUM_BUCKETS - 1)
    return np.where(dist < max_exact, dist, large).astype(np.int32)

def mla_attention(q, k, v):
    B, S, H, _ = q.shape
    nblk = S // Q_BLOCK
    scale = 1.0 / math.sqrt(MLA_QK_DIM)
    qb = q.reshape(B, nblk, Q_BLOCK, H, MLA_QK_DIM).transpose(1, 0, 2, 3, 4)
    starts = jnp.arange(nblk, dtype=jnp.int32) * Q_BLOCK
    kpos = jnp.arange(S, dtype=jnp.int32)

    def one_block(args):
        q_blk, start = args
        s = jnp.einsum('bqhd,bkhd->bhqk', q_blk, k).astype(jnp.float32) * scale
        qpos = start + jnp.arange(Q_BLOCK, dtype=jnp.int32)
        s = jnp.where(kpos[None, :] <= qpos[:, None], s, NEG_INF)
        p = jax.nn.softmax(s, axis=-1)
        return jnp.einsum('bhqk,bkhd->bqhd', p.astype(v.dtype), v)

    out = lax.map(one_block, (qb, starts))
    return out.transpose(1, 0, 2, 3, 4).reshape(B, S, H * MLA_V_DIM)

def swa_attention(q, k, v, sinks, rel_bias):
    B, S = q.shape[:2]
    nblk = S // Q_BLOCK
    scale = 1.0 / math.sqrt(SWA_HEAD_DIM)
    qb = q.reshape(B, nblk, Q_BLOCK, SWA_KV_HEADS, SWA_GROUP, SWA_HEAD_DIM)

    def band(t):
        tb = t.reshape(B, nblk, Q_BLOCK, SWA_KV_HEADS, SWA_HEAD_DIM)
        prev = jnp.pad(tb, ((0, 0), (1, 0), (0, 0), (0, 0), (0, 0)))[:, :-1]
        return jnp.concatenate([prev, tb], axis=2)

    kb, vb = band(k), band(v)
    s = jnp.einsum('bnqhgd,bnkhd->bnhgqk', qb, kb).astype(jnp.float32) * scale
    i = np.arange(Q_BLOCK)[:, None]
    j = np.arange(2 * Q_BLOCK)[None, :]
    dist = i + Q_BLOCK - j
    in_window = (dist >= 0) & (dist < WINDOW)
    blk = np.arange(nblk)[:, None, None]
    valid = in_window[None] & (blk * Q_BLOCK + j[None] - Q_BLOCK >= 0)
    bias = rel_bias.astype(jnp.float32)[t5_causal_bucket(dist)]
    bias = bias.reshape(Q_BLOCK, 2 * Q_BLOCK, SWA_KV_HEADS, SWA_GROUP).transpose(2, 3, 0, 1)
    s = jnp.where(valid[None, :, None, None], s + bias[None, None], NEG_INF)
    sink = sinks.astype(jnp.float32).reshape(SWA_KV_HEADS, SWA_GROUP)[None, None, :, :, None, None]
    m = jnp.maximum(jnp.max(s, axis=-1, keepdims=True), sink)
    p = jnp.exp(s - m)
    probs = p / (jnp.sum(p, axis=-1, keepdims=True) + jnp.exp(sink - m))
    out = jnp.einsum('bnhgqk,bnkhd->bnqhgd', probs.astype(v.dtype), vb)
    return out.reshape(B, S, SWA_HEADS * SWA_HEAD_DIM)

def setup_inputs(seed: int = 0) -> dict:
    key = jax.random.key(seed)
    ks = jax.random.split(key, 20)
    f32 = jnp.float32

    def w(k, shape, fan_in):
        return jax.random.normal(k, shape, f32) * fan_in ** -0.5

    def gain(k, shape):
        return 1.0 + 0.05 * jax.random.normal(k, shape, f32)

    x = jax.random.normal(ks[0], (BATCH, SEQ, D_MODEL), f32)
    positions = jnp.broadcast_to(jnp.arange(SEQ, dtype=jnp.int32)[None, :], (BATCH, SEQ))
    return {
        "x": x,
        "positions": positions,
        "g_mix_pre": gain(ks[1], (DEPTH, D_MODEL)),
        "w_in": w(ks[2], (DEPTH, D_MODEL, IN_WIDTH), D_MODEL),
        "g_cq": gain(ks[3], (DEPTH, Q_LORA_RANK)),
        "g_ckv": gain(ks[4], (DEPTH, KV_LORA_RANK)),
        "w_uq": w(ks[5], (DEPTH, Q_LORA_RANK, MLA_HEADS * MLA_QK_DIM), Q_LORA_RANK),
        "w_ukv": w(ks[6], (DEPTH, KV_LORA_RANK, MLA_HEADS * (MLA_NOPE_DIM + MLA_V_DIM)), KV_LORA_RANK),
        "sinks": 0.5 * jax.random.normal(ks[7], (DEPTH, SWA_HEADS), f32),
        "rel_bias": 0.5 * jax.random.normal(ks[8], (NUM_BUCKETS, SWA_HEADS), f32),
        "w_o": w(ks[9], (DEPTH, MIX_WIDTH, D_MODEL), MIX_WIDTH),
        "g_mix_post": gain(ks[10], (DEPTH, D_MODEL)),
        "g_ffn_pre": gain(ks[11], (DEPTH, D_MODEL)),
        "w_gate": w(ks[12], (DEPTH, D_MODEL, D_FF), D_MODEL),
        "w_up": w(ks[13], (DEPTH, D_MODEL, D_FF), D_MODEL),
        "w_down": w(ks[14], (DEPTH, D_FF, D_MODEL), D_FF),
        "g_ffn_post": gain(ks[15], (DEPTH, D_MODEL)),
    }

def reference(x, positions, g_mix_pre, w_in, g_cq, g_ckv, w_uq, w_ukv, sinks, rel_bias,
              w_o, g_mix_post, g_ffn_pre, w_gate, w_up, w_down, g_ffn_post):
    B, S, _ = x.shape
    split_idx = [int(c) for c in np.cumsum(IN_SIZES)[:-1]]
    for layer in range(DEPTH):
        h = rms_norm(x, g_mix_pre[layer])
        proj = h @ w_in[layer]
        c_q, c_kv, k_r, sq, sk, sv = jnp.split(proj, split_idx, axis=-1)

        c_q = rms_norm(c_q, g_cq[layer])
        c_kv = rms_norm(c_kv, g_ckv[layer])
        q = (c_q @ w_uq[layer]).reshape(B, S, MLA_HEADS, MLA_QK_DIM)
        q = jnp.concatenate([q[..., :MLA_NOPE_DIM], rope(q[..., MLA_NOPE_DIM:], positions)], axis=-1)
        kv = (c_kv @ w_ukv[layer]).reshape(B, S, MLA_HEADS, MLA_NOPE_DIM + MLA_V_DIM)
        k_nope, v_a = kv[..., :MLA_NOPE_DIM], kv[..., MLA_NOPE_DIM:]
        k_rope = rope(k_r[:, :, None, :], positions)
        k_a = jnp.concatenate(
            [k_nope, jnp.broadcast_to(k_rope, (B, S, MLA_HEADS, MLA_ROPE_DIM))], axis=-1)
        out_a = mla_attention(q, k_a, v_a)

        out_b = swa_attention(sq.reshape(B, S, SWA_HEADS, SWA_HEAD_DIM),
                              sk.reshape(B, S, SWA_KV_HEADS, SWA_HEAD_DIM),
                              sv.reshape(B, S, SWA_KV_HEADS, SWA_HEAD_DIM),
                              sinks[layer], rel_bias)

        mix = jnp.concatenate([out_a, out_b], axis=-1) @ w_o[layer]
        x = x + rms_norm(mix, g_mix_post[layer])

        h = rms_norm(x, g_ffn_pre[layer])
        ff = (jax.nn.silu(h @ w_gate[layer]) * (h @ w_up[layer])) @ w_down[layer]
        x = x + rms_norm(ff, g_ffn_post[layer])
    return x


_drawn_inputs = setup_inputs


def setup_inputs(seed=0):
    import zlib

    import numpy as np

    out = dict(_drawn_inputs(seed))
    spreads = {}
    factors = {'sinks': 8.0}
    for name, (base, spread) in spreads.items():
        noise = np.random.default_rng([zlib.crc32(name.encode()), seed]).standard_normal(out[name].shape)
        drawn = base * np.exp(spread * noise) if base else spread * noise
        out[name] = __import__('jax').numpy.asarray(drawn.astype(out[name].dtype))
    for name, factor in factors.items():
        out[name] = (out[name] * factor).astype(out[name].dtype)
    return out
```

```python
import math
from contextlib import ExitStack

import numpy as np

import concourse.bass as bass
from concourse import mybir

F32 = mybir.dt.float32
F32R = mybir.dt.float32r
I32 = mybir.dt.int32
ALU = mybir.AluOpType
ACT = mybir.ActivationFunctionType
AX = mybir.AxisListType

P = 128
D = 2048
S = 512
DFF = 5632
TB = S // P
KD = D // P
LORA = 512
KL = LORA // P
MLA_HEADS = 8
NOPE = 128
ROPE = 64
VDIM = 128
SWA_HEADS = 16
SWA_DIM = 64
WINDOW = 128
NUM_BUCKETS = 32
MAX_DISTANCE = 128
ROPE_THETA = 10000.0
EPS = 1e-6
NEG = -1e30
MLA_SCALE = 1.0 / math.sqrt(NOPE + ROPE)
SWA_SCALE = 1.0 / math.sqrt(SWA_DIM)

C_Q, C_KV, C_KR, C_SQ = 0, 512, 1024, 1088
C_SK = C_SQ + SWA_HEADS * SWA_DIM
C_SV = C_SK + 128
IN_PANELS = ([("ckv", j, C_KV + P * j) for j in range(KL)] + [("cq", j, C_Q + P * j) for j in range(KL)]
             + [("kr", 0, C_KR), ("sk", 0, C_SK), ("sv", 0, C_SV)]
             + [("sq", j, C_SQ + P * j) for j in range(8)])
N_IN = len(IN_PANELS)
PAIRS = MLA_HEADS // 2
Q_MLA = N_IN
Q_OUT = Q_MLA + 2 * PAIRS
Q_FFN = Q_OUT + 16
BLOCKS = DFF // 512
PER_BLOCK = 12
Q_END = Q_FFN + PER_BLOCK * BLOCKS
KG_ORDER = [2, 3, 0, 1]
CHUNK_BANKS = 6
AHEAD = 4
BIAS_W = 384
PT_W = 512 + 384 + 512
TWO_PI = 2.0 * math.pi
MAGIC = 12582912.0


def two_pi_pieces():
    point = 120
    rest = (31415926535897932384626433832795028841971 << point) // (5 * 10 ** 39)
    out = []
    for _ in range(4):
        shift = rest.bit_length() - 12
        out.append(float(rest >> shift) * 2.0 ** (shift - point))
        rest &= (1 << shift) - 1
    return out


def bucket_rows():
    dist = 255 - np.arange(BIAS_W)
    d = np.maximum(dist, 0)
    half = NUM_BUCKETS // 2
    large = half + (np.log(np.maximum(d, 1) / half) / np.log(MAX_DISTANCE / half)
                    * (NUM_BUCKETS - half)).astype(np.int32)
    bucket = np.where(d < half, d, np.minimum(large, NUM_BUCKETS - 1))
    valid = (dist >= 0) & (dist < WINDOW)
    rows = np.zeros((NUM_BUCKETS + 1, BIAS_W), np.float32)
    rows[bucket[valid], np.arange(BIAS_W)[valid]] = 1.0
    rows[NUM_BUCKETS, ~valid] = NEG
    return rows


def inverse_frequencies():
    half = ROPE // 2
    f = np.float32(ROPE_THETA) ** (-np.arange(half, dtype=np.float32) / np.float32(half))
    return np.tile(f.astype(np.float32), P // half)[:, None]


def build(nc, x, positions, g_mix_pre, w_in, g_cq, g_ckv, w_uq, w_ukv, sinks, rel_bias, w_o,
          g_mix_post, g_ffn_pre, w_gate, w_up, w_down, g_ffn_post, buckets, inv_freq, out):
    ctx = ExitStack()
    with ctx:
        base = nc.sbuf_base + 31 & ~31

        def sb(name, kb, shape, dt=F32):
            return nc.alloc_sbuf_tensor_at(name, shape, dt, offset=base + int(kb * 1024))

        def sem(name):
            return ctx.enter_context(nc.semaphore(name))

        assert nc.sbuf_top - base >= 207 * 1024
        raw = [sb(f"raw{i}", 8 * i, [P, 2048]) for i in range(2)]
        whi = [sb(f"whi{i}", 16 + 8 * i, [P, 2048], F32R) for i in range(2)]
        wlo = [sb(f"wlo{i}", 32 + 8 * i, [P, 2048], F32R) for i in range(2)]
        ident = sb("ident", 48, [P, P])
        rot = sb("rot", 48.5, [P, P])
        ones = sb("ones", 49, [P, P])
        small = sb("small", 49.5, [P, 112])
        cos_t = sb("cos_t", 50, [P, S])
        sin_t = sb("sin_t", 52, [P, S])

        at = [0]

        def cols(n):
            at[0] += n
            assert at[0] <= 112
            return small[:, at[0] - n:at[0]]

        N_GAIN = 2 * KD + 2 * KL
        gains = cols(N_GAIN)
        gpre, gffn = gains[:, 0:KD], gains[:, KD:2 * KD]
        gckv, gcq = gains[:, 2 * KD:2 * KD + KL], gains[:, 2 * KD + KL:]
        invf = cols(1)
        sink8 = cols(SWA_HEADS)
        ssum, mean, root, y0, yy, cc_, rstd = (cols(TB) for _ in range(7))
        st = sb("st", 206, [P, 3, 6, 4])
        ss4 = sb("ss4", 206.5, [P, TB, 4])

        act_hi0 = sb("act_hi0", 54, [P, KD, S], F32R)
        act_lo0 = sb("act_lo0", 86, [P, KD, S], F32R)
        xin = sb("xin", 118, [P, TB, D])
        junk0 = sb("junk0", 150, [P, D])
        relaug = sb("relaug", 162, [NUM_BUCKETS + 1, 16])
        bsel = sb("bsel", 163, [NUM_BUCKETS + 1, BIAS_W])
        brow = sb("brow", 165, [16, BIAS_W])
        gpre_rows = sb("gpre_rows", 167, [KD, P])
        gain_rows = sb("gain_rows", 167.5, [N_GAIN - KD, P])
        pos_i = sb("pos_i", 162, [P, S], I32)
        ang, kk, kh = (sb(n, 164 + 2 * i, [P, S]) for i, n in enumerate(("ang", "kk", "kh")))
        w_ms, w_y, w_a = (sb(n, 170 + 2 * i, [P, S]) for i, n in enumerate(("w_ms", "w_y", "w_a")))
        rcol0 = sb("rcol0", 176, [P, TB, P])
        rrow0 = sb("rrow0", 160, [P, S])
        ckv = [sb("ckv_hi", 118, [P, KL, S], F32R), sb("ckv_lo", 126, [P, KL, S], F32R)]
        cq = [sb("cq_hi", 134, [P, KL, S], F32R), sb("cq_lo", 142, [P, KL, S], F32R)]
        craw = [sb("craw_kv", 150, [P, KL, S]), sb("craw_q", 162, [P, KL, S])]
        skd = sb("skd", 150, [P, 2, S])
        svt = sb("svt", 154, [P, S])
        kraw = sb("kraw", 158, [P, S])
        sqt = sb("sqt", 176, [P, S])
        sq = sb("sq", 162, [P, 8, S])
        kpad = [sb("kpad_hi", 178, [P, 2, 2, S], F32R), sb("kpad_lo", 186, [P, 2, 2, S], F32R)]
        vpad = [sb("vpad_hi", 194, [P, TB, 2, 192], F32R), sb("vpad_lo", 200, [P, TB, 2, 192], F32R)]
        mix_s = sb("mix_s", 54, [P, 8, S])
        spt = [[sb(f"spt{b}_hi", 70 + 8 * b, [P, 2, 512], F32R), sb(f"spt{b}_lo", 74 + 8 * b, [P, 2, 512], F32R)]
               for b in range(2)]
        qs = [[sb(f"qs{b}_hi", kb, [P, 2, S], F32R), sb(f"qs{b}_lo", kb + 4, [P, 2, S], F32R)]
              for b, kb in enumerate((150, 94))]
        bias_t = [sb(f"bias{b}", 102 + 4 * b, [P, 4, 256]) for b in range(2)]
        sp = [sb(f"sp{b}", kb, [P, 4, 256]) for b, kb in enumerate((110, 114, 86))]
        qn = [sb("qn_hi", 70, [P, 2, S], F32R), sb("qn_lo", 74, [P, 2, S], F32R)]
        kn = [sb("kn_hi", 78, [P, 2, S], F32R), sb("kn_lo", 82, [P, 2, S], F32R)]
        vn = [sb("vn_hi", 86, [P, TB, 256], F32R), sb("vn_lo", 90, [P, TB, 256], F32R)]
        qr = [sb("qr_hi", 94, [P, S], F32R), sb("qr_lo", 96, [P, S], F32R)]
        mix_m = sb("mix_m", 98, [P, 8, S])
        tri = sb("tri", 114, [P, S])
        t_sb = sb("t_sb", 197, [P, S])
        t_a = sb("t_a", 199, [P, S])
        t_b = sb("t_b", 201, [P, S])
        mpt = [[sb("mpt0_hi", 150, [P, PT_W], F32R), sb("mpt0_lo", 155.5, [P, PT_W], F32R)],
               [sb("mpt1_hi", 186, [P, PT_W], F32R), sb("mpt1_lo", 191.5, [P, PT_W], F32R)]]
        krp = [sb("krp_hi", 162, [P, 2, S], F32R), sb("krp_lo", 166, [P, 2, S], F32R)]
        mp = [sb(f"mp{b}", 170 + 8 * b, [P, TB, S]) for b in range(2)]
        mixt = [sb("mixt_hi", 118, [P, KD, S], F32R), sb("mixt_lo", 150, [P, KD, S], F32R)]
        mixn = sb("mixn", 54, [P, TB, D])
        x1 = sb("x1", 86, [P, TB, D])
        gpost = sb("gpost", 182, [P, D])
        junk4 = sb("junk4", 190, [P, D])
        act_hi = sb("act_hi", 118, [P, KD, S], F32R)
        act_lo = sb("act_lo", 150, [P, KD, S], F32R)
        acc = sb("acc", 54, [P, TB, D])
        gt = [sb("gt_hi", 182, [P, 4, S], F32R), sb("gt_lo", 190, [P, 4, S], F32R)]
        sil = sb("sil", 198, [P, S])
        gf = sb("gf", 200, [P, S])
        junk6 = sb("junk6", 202, [P, S])
        rcol = sb("rcol", 202, [P, TB, P])
        rrow = sb("rrow", 204, [P, S])

        pt_ = [ctx.enter_context(nc.psum_tensor(f"bank{i}", [P, 512], F32)) for i in range(8)]
        bank = [t[:, :] for t in pt_]

        bias_row = nc.dram_tensor("bias_row", (16, BIAS_W), F32, kind="Internal").ap()
        bias_all = nc.dram_tensor("bias_all", (P, 16 * BIAS_W), F32, kind="Internal").ap()

        x_in = [sem(f"x_in{c}") for c in range(4)]
        raw_in = [sem(f"raw_in{i}") for i in range(2)]
        x_again = sem("x_again")
        y_out = sem("y_out")
        bias_src_in = sem("bias_src_in")
        cols_in = sem("cols_in")
        gpre_in = sem("gpre_in")
        rows_in = sem("rows_in")
        row_out = sem("row_out")
        rows_out = sem("rows_out")
        pos_in = sem("pos_in")
        band_in = [sem(f"band_in{b}") for b in range(2)]
        gpost_in = sem("gpost_in")
        made = sem("made")
        made_m = sem("made_m")
        acc_zero = sem("acc_zero")
        x1_pool = sem("x1_pool")
        s_norm = sem("s_norm")
        y_pool = sem("y_pool")
        hi_ready = sem("hi_ready")
        sumsq_x = sem("sumsq_x")
        root_done = sem("root_done")
        squares = sem("squares")
        sines = sem("sines")
        act_h = sem("act_h")
        q_hi = sem("q_hi")
        s_exp = sem("s_exp")
        s_hi = sem("s_hi")
        s_out = sem("s_out")
        m_exp = sem("m_exp")
        m_hi = sem("m_hi")
        m_out = sem("m_out")
        o_sq = sem("o_sq")
        scaled = sem("scaled")
        silu_done = sem("silu_done")
        g_hi = sem("g_hi")
        lo_ready = sem("lo_ready")
        link_s = sem("link_s")
        brow_ready = sem("brow_ready")
        gain_cols = sem("gain_cols")
        mean_done = sem("mean_done")
        rcol_ready = sem("rcol_ready")
        rrow_ready = sem("rrow_ready")
        act_l = sem("act_l")
        angle_done = sem("angle_done")
        taken = sem("taken")
        normed = sem("normed")
        q_lo = sem("q_lo")
        s_max = sem("s_max")
        s_reci = sem("s_reci")
        s_lo = sem("s_lo")
        r_in = sem("r_in")
        r_done = sem("r_done")
        m_max = sem("m_max")
        m_neg = sem("m_neg")
        m_norm = sem("m_norm")
        m_lo = sem("m_lo")
        o_taken = sem("o_taken")
        rstd_ready = sem("rstd_ready")
        x1_ready = sem("x1_ready")
        sil_normed = sem("sil_normed")
        gated = sem("gated")
        gained = sem("gained")
        g_done = sem("g_done")
        g_lo = sem("g_lo")
        y_ready = sem("y_ready")
        bias_mm = sem("bias_mm")
        gains_mm = sem("gains_mm")
        tr = sem("tr")
        rrow_mm = sem("rrow_mm")
        used = sem("used")
        sumsq_c = sem("sumsq_c")
        sv_t = sem("sv_t")
        s_qk = sem("s_qk")
        s_t = sem("s_t")
        s_pv = sem("s_pv")
        m_proj = sem("m_proj")
        r_perm = sem("r_perm")
        m_qk = sem("m_qk")
        m_t = sem("m_t")
        m_pv = sem("m_pv")
        o_bank = sem("o_bank")
        d_bank = sem("d_bank")

        x_v = x[0].rearrange("(t p) n -> t p n", p=P)
        x_cols = x[0].rearrange("(t p) n -> p t n", p=P)
        out_v = out[0].rearrange("(t p) n -> t p n", p=P)
        win_v = w_in[0].rearrange("(k p) n -> p k n", p=P)
        wuq_v = w_uq[0].rearrange("(k p) n -> p k n", p=P)
        wukv_v = w_ukv[0].rearrange("(k p) n -> p k n", p=P)
        wo_v = w_o[0].rearrange("(k p) n -> p k n", p=P)
        wg_v = w_gate[0].rearrange("(k p) n -> p k n", p=P)
        wu_v = w_up[0].rearrange("(k p) n -> p k n", p=P)
        wd_v = w_down[0].rearrange("(m p) n -> p m n", p=P)
        band_v = bias_all.rearrange("p (h w) -> p h w", h=16)

        def k16(t):
            return t[:, :].rearrange("p (k n) -> p k n", k=KD)

        def k4(t, n=512):
            return t[:, 0:4 * n].rearrange("p (k n) -> p k n", k=4)

        def split_parts(q, slot):
            if not (isinstance(q, int) and Q_MLA <= q < Q_OUT and (q - Q_MLA) % 2):
                return [(whi[slot][:, :], raw[slot][:, :], wlo[slot][:, :])]
            src = k4(raw[slot], 384).rearrange("p k (h n) -> p k h n", h=2)
            out_ = []
            for c0, w, a in ((0, NOPE, 0), (NOPE, ROPE, 2 * NOPE)):
                hi, lo = (k4(t, 384)[:, :, a:a + 2 * w].rearrange("p k (h n) -> p k h n", h=2)
                          for t in (whi[slot], wlo[slot]))
                out_.append((hi, src[:, :, :, c0:c0 + w], lo))
            return out_

        def f(ap):
            return ap.bitcast(F32)

        N_H0 = KD
        N_CKV = N_H0 + KL
        N_CQ = N_CKV + KL
        N_SK = N_CQ + 4
        N_SV = N_SK + 1
        N_KR = N_SV + 2
        PER_PAIR = 7
        PROJ = 5
        PT_PARTS = ((0, 512), (512, 384), (896, 512))
        N_PAIRS = N_KR + PER_PAIR * PAIRS
        N_MIX = N_PAIRS + KD
        MIX_ORDER = [4 * kg + k for kg in KG_ORDER for k in range(4)]
        O_BASE = 16
        UNITS = 16

        def split_hi(q, slot):
            nc.scalar.wait_ge(raw_in[slot], (q - slot) * 8 + 16)
            if not isinstance(q, int) or q >= 2:
                nc.scalar.wait_ge(used, q - 1)
            for dst, src, _ in split_parts(q, slot):
                last = nc.scalar.activation(dst, src, ACT.Copy)
            last.then_inc(hi_ready, 1)

        def split_lo(q, slot):
            nc.vector.wait_ge(hi_ready, q + 1)
            for hi, src, dst in split_parts(q, slot):
                last = nc.vector.tensor_tensor(dst, src, f(hi), ALU.subtract)
            last.then_inc(lo_ready, 1)

        def stat(u, kind):
            return st[:, u % 3, kind, :]

        MAXI, NEGM, SINKN, SINKE, TOTAL, RECI = range(6)

        def unit(u):
            return u // 4, u // 8, u % 4, (P if u % 4 == 0 else 0)

        def halves(u):
            first = 2 * u - (u + 3) // 4
            return [(kb, first + m) for m, kb in enumerate((1,) if u % 4 == 0 else (0, 1))]

        N_HALVES = halves(UNITS - 1)[-1][1] + 1

        def half_bank(h):
            return bank[4 + h % 3]

        def mix_chunk(c):
            return mix_m[:, c, :] if c < 8 else mix_s[:, c - 8, :]

        def in_bank(q):
            return bank[(0, 1, 5)[q % 3]]

        def chunk_bank(c):
            return bank[1 + c % CHUNK_BANKS]

        def residual(src, t, a):
            return nc.vector.scalar_tensor_tensor(out=x1[:, t, a], in0=src[:, t, a], scalar=rstd[:, t:t + 1],
                                                  in1=x1[:, t, a], op0=ALU.mult, op1=ALU.add)

        def residual_times(src, t, a):
            return nc.scalar.activation(src[:, t, a], src[:, t, a], ACT.Copy, scale=rstd[:, t:t + 1])

        def residual_plus(src, t, a):
            return nc.gpsimd.tensor_tensor(x1[:, t, a], x1[:, t, a], src[:, t, a], ALU.add)

        def shared(t):
            return slice(0, 1024 if t < TB - 1 else 512)

        def three(out_ap, a, b, first, last):
            nc.tensor.matmul(out_ap, a[0], b[0], start=first, stop=False)
            nc.tensor.matmul(out_ap, a[0], b[1], start=False, stop=False)
            return nc.tensor.matmul(out_ap, a[1], b[0], start=False, stop=last)

        block = ctx.enter_context(nc.Block())

        @block.sync
        def _(sp_):
            def fetch(q, src, view):
                if q >= 2:
                    sp_.wait_ge(lo_ready, q - 1)
                sp_.dma_start(view, src).then_inc(raw_in[q % 2], 16)

            for q, (_, _, c) in enumerate(IN_PANELS):
                fetch(q, win_v[:, :, c:c + P], k16(raw[q % 2]))
                if q == 0:
                    for n in range(4):
                        cols_n = slice(512 * n, 512 * n + 512)
                        sp_.dma_start(xin[:, :, cols_n], x_cols[:, :, cols_n]).then_inc(x_in[n], 16)
            for p in range(PAIRS):
                q = Q_MLA + 2 * p
                fetch(q, wukv_v[:, :, 512 * p:512 * p + 512], k4(raw[q % 2]))
                fetch(q + 1, wuq_v[:, :, 384 * p:384 * p + 384], k4(raw[(q + 1) % 2], 384))
            for i in range(16):
                q = Q_OUT + i
                cb, kg = i // 4, KG_ORDER[i % 4]
                fetch(q, wo_v[:, 4 * kg:4 * kg + 4, 512 * cb:512 * cb + 512], k4(raw[q % 2]))
                if i == 3:
                    sp_.wait_ge(act_l, N_MIX)
                    for t in range(TB):
                        sp_.dma_start(x1[:, t, :], x_v[t]).then_inc(x_again, 16)

            def fetch_block(b):
                for j in range(PER_BLOCK):
                    slot = (Q_FFN + j) % 2
                    sp_.wait_ge(lo_ready, b * PER_BLOCK + (Q_FFN + j - 1))
                    if j < 8:
                        src = (wg_v, wu_v)[j % 2][:, :, bass.ds(b * 512 + P * (j // 2), P)]
                        sp_.dma_start(k16(raw[slot]), src).then_inc(raw_in[slot], 16)
                    else:
                        src = wd_v[:, bass.ds(b * 4, 4), 512 * (j - 8):512 * (j - 8) + 512]
                        sp_.dma_start(k4(raw[slot]), src).then_inc(raw_in[slot], 16)

            with sp_.Fori(0, BLOCKS - 1) as b:
                fetch_block(b)
            fetch_block(BLOCKS - 1)
            sp_.wait_ge(lo_ready, Q_END - 1)
            sp_.dma_start(raw[Q_END % 2][:, :], g_ffn_post.broadcast_to([P, D])).then_inc(raw_in[Q_END % 2], 16)
            for t in range(TB):
                sp_.wait_ge(y_ready, t + 1)
                w = shared(t).stop
                sp_.dma_start(out_v[t][:, w:D], x1[:, t, w:D]).then_inc(y_out, 16)
                sp_.wait_ge(y_pool, t + 1)
                sp_.dma_start(out_v[t][:, 0:w], x1[:, t, 0:w]).then_inc(y_out, 16)
            sp_.wait_ge(y_out, 16 * 2 * TB)

        @block.gpsimd
        def _(pool):
            n = [0]

            def make(ins):
                n[0] += 1
                ins.then_inc(made, 1)

            make(nc.gpsimd.memset(ident[:, :], 0.0))
            make(nc.gpsimd.memset(rot[:, :], 0.0))
            make(nc.gpsimd.memset(ones[:, :], 1.0))
            pool.wait_ge(made, 3)
            make(nc.gpsimd.memset(relaug[NUM_BUCKETS:NUM_BUCKETS + 1, :], 1.0))
            pool.wait_ge(made, 4)
            make(nc.gpsimd.affine_select(out=ident[:, :], in_=ident[:, :], compare_op=ALU.not_equal, fill=1.0,
                                         base=0, pattern=[[-1, P]], channel_multiplier=1))
            rv = rot[:, :].rearrange("p (b h r) -> p b h r", b=2, h=2)
            make(nc.gpsimd.affine_select(out=rv[:, :, 0, :], in_=rv[:, :, 0, :], compare_op=ALU.not_equal,
                                         fill=-1.0, base=-32, pattern=[[-64, 2], [-1, 32]], channel_multiplier=1))
            pool.wait_ge(made, 6)
            make(nc.gpsimd.affine_select(out=rv[:, :, 1, :], in_=rv[:, :, 1, :], compare_op=ALU.not_equal,
                                         fill=1.0, base=0, pattern=[[-64, 2], [-1, 32]], channel_multiplier=1))
            for t in (*kpad, *vpad):
                make(nc.gpsimd.memset(f(t[:]), 0.0))
            for u in range(UNITS):
                lo = unit(u)[3]
                pool.wait_ge(s_reci, u + 1)
                blk = sp[u % 3][:, :, lo:256]
                nc.gpsimd.tensor_tensor(blk, blk, stat(u, RECI).unsqueeze(2).broadcast_to([P, 4, 256 - lo]),
                                        ALU.mult).then_inc(s_norm, 1)
            pool.wait_ge(s_out, UNITS)
            pool.wait_ge(used, N_IN)
            nc.gpsimd.memset(tri[:, :], 0.0).then_inc(made_m, 1)
            pool.wait_ge(made_m, 1)
            nc.gpsimd.affine_select(out=tri[:, 384:512], in_=tri[:, 384:512], compare_op=ALU.is_ge, fill=NEG,
                                    base=0, pattern=[[-1, P]], channel_multiplier=1).then_inc(made_m, 1)
            for t in krp:
                nc.gpsimd.memset(f(t[:]), 0.0).then_inc(made_m, 1)
            for t in mp:
                nc.gpsimd.memset(t[:, 2, 384:512], 0.0).then_inc(made_m, 1)
            pool.wait_ge(x_again, 16 * TB)
            for t in range(TB):
                for n in (2, 3):
                    pool.wait_ge(scaled, 2 * t + n - 1)
                    residual_plus(mixn, t, slice(512 * n, 512 * n + 512)).then_inc(x1_pool, 1)
            pool.wait_ge(x1_ready, 2 * TB)
            pool.wait_ge(x1_pool, 2 * TB)
            nc.gpsimd.memset(acc[:], 0.0).then_inc(acc_zero, 1)
            for t in range(TB):
                pool.wait_ge(scaled, 2 * TB + t + 1)
                residual_plus(acc, t, shared(t)).then_inc(y_pool, 1)

        @block.scalar
        def _(act):
            def copy_hi(dst, src, scale=None):
                if scale is None:
                    nc.scalar.activation(dst, src, ACT.Copy).then_inc(act_h, 1)
                else:
                    nc.scalar.activation(dst, src, ACT.Copy, scale=scale).then_inc(act_h, 1)

            def token_squares(src, junk):
                for t in range(TB):
                    if sumsqs[0]:
                        act.wait_ge(sumsq_x, sumsqs[0])
                    nc.scalar.activation(junk[:, :], src[:, t, :], ACT.Square,
                                         accum_out=ssum[:, t:t + 1]).then_inc(sumsq_x, 1)
                    sumsqs[0] += 1

            sumsqs = [0]

            act.dma_start(gpre_rows[:, :], g_mix_pre[0].rearrange("(c p) -> c p", p=P)).then_inc(gpre_in, 16)
            at_row = 0
            for src in (g_ffn_pre, g_ckv, g_cq):
                rows = src[0].rearrange("(c p) -> c p", p=P)
                act.dma_start(gain_rows[at_row:at_row + rows.shape[0], :], rows).then_inc(rows_in, 16)
                at_row += rows.shape[0]
            act.dma_start(relaug[0:NUM_BUCKETS, :], rel_bias).then_inc(bias_src_in, 16)
            act.dma_start(bsel[:, :], buckets).then_inc(bias_src_in, 16)
            act.dma_start(invf, inv_freq).then_inc(cols_in, 16)
            act.dma_start(sink8, sinks.broadcast_to([P, SWA_HEADS])).then_inc(cols_in, 16)

            act.wait_ge(made, 3)
            nc.scalar.activation(ss4[:, 0, 0:1], ones[:, 0:1], ACT.Copy)
            split_hi(0, 0)
            act.wait_ge(gain_cols, 1)
            for c in range(KD):
                if c == 12:
                    split_hi(1, 1)
                act.wait_ge(tr, c + 1)
                copy_hi(act_hi0[:, c, :], chunk_bank(c), gpre[:, c:c + 1])
            for n in range(4):
                act.wait_ge(x_in[n], 16)
            token_squares(xin, junk0)
            act.wait_ge(mean_done, 1)
            nc.scalar.activation(root[:, :], mean[:, :], ACT.Sqrt).then_inc(root_done, 1)
            split_hi(2, 0)
            act.wait_ge(brow_ready, 1)
            act.dma_start(bias_row, brow[:, :]).then_inc(row_out, 16)
            act.wait_ge(row_out, 16)
            act.dma_start(bias_all, bias_row.rearrange("h w -> (h w)").unsqueeze(0)
                          .broadcast_to([P, 16 * BIAS_W])).then_inc(rows_out, 16)
            act.dma_start(pos_i[:, :], positions.broadcast_to([P, S])).then_inc(pos_in, 16)

            def split_queries_hi(gh):
                nc.scalar.activation(qs[gh % 2][0][:, :, :], sq[:, 2 * gh:2 * gh + 2, :],
                                     ACT.Copy).then_inc(q_hi, 1)

            for q in range(N_IN):
                what, j, _ = IN_PANELS[q]
                if what in ("ckv", "cq"):
                    act.wait_ge(taken, q + 1)
                    if q:
                        act.wait_ge(sumsq_c, q)
                    nc.scalar.activation(sqt[:, :], craw[q // KL][:, j, :], ACT.Square).then_inc(squares, 1)
                if q:
                    split_hi(q + 2, q % 2)
                if q == 2:
                    act.wait_ge(angle_done, 1)
                    nc.scalar.activation(sin_t[:, :], ang[:, :], ACT.Sin).then_inc(sines, 1)
                    nc.scalar.activation(kk[:, :], ang[:, :], ACT.Sin, scale=0.5).then_inc(sines, 1)
                if q in (KL, 2 * KL):
                    n = q // KL - 1
                    act.wait_ge(mean_done, n + 2)
                    nc.scalar.activation(w_y[:, :], w_ms[:, :], ACT.Sqrt).then_inc(root_done, 1)
                    for i in range(KL):
                        act.wait_ge(normed, KL * n + i + 1)
                        copy_hi((ckv, cq)[n][0][:, i, :], craw[n][:, i, :])
                if what == "sk":
                    act.wait_ge(made, 11)
                    act.wait_ge(taken, q + 1)
                    for i in range(4):
                        g, e = i // 2, i % 2
                        rows = slice(64 * e, 64 * e + 64)
                        copy_hi(kpad[0][rows, g, e, :], skd[rows, g, :])
                if q == N_IN - 4:
                    act.wait_ge(taken, N_IN - 6)
                    split_queries_hi(0)
                if q == N_IN - 8:
                    act.wait_ge(sv_t, 1)
                    copy_hi(vpad[0][:, :, :, 64:128], bank[4].rearrange("p (b g d) -> p b g d", b=TB, g=2))

            act.wait_ge(used, N_IN)

            def load_band(gh):
                act.dma_start(bias_t[gh % 2][:, :, :],
                              bass.AP(tensor=bias_all.tensor, offset=4 * gh * BIAS_W + 127,
                                      ap=[[16 * BIAS_W - 1, P], [BIAS_W, 4], [1, 256]])
                              ).then_inc(band_in[gh % 2], 16)

            act.wait_ge(rows_out, 16)
            load_band(0)
            load_band(1)
            for s in range(UNITS + 4):
                if s >= 4:
                    u = s - 4
                    gh, _, n, _ = unit(u)
                    act.wait_ge(s_pv, u + 1)
                    nc.scalar.activation(mix_s[:, 2 * gh:2 * gh + 2, P * n:P * n + P],
                                         bank[7][:, 0:256].rearrange("p (c n) -> p c n", c=2),
                                         ACT.Copy).then_inc(s_out, 1)
                if 2 <= s < UNITS + 2:
                    u = s - 2
                    if u >= 2:
                        act.wait_ge(s_pv, u - 1)
                    for kb, h in halves(u):
                        act.wait_ge(s_t, h + 1)
                        nc.scalar.activation(spt[u % 2][0][:, kb, :], half_bank(h), ACT.Copy).then_inc(s_hi, 1)
                if s < UNITS:
                    gh, _, n, lo = unit(s)
                    act.wait_ge(s_max, s + 1)
                    for hd in range(4):
                        nc.scalar.activation(sp[s % 3][:, hd, lo:256], sp[s % 3][:, hd, lo:256], ACT.Exp,
                                             bias=stat(s, NEGM)[:, hd:hd + 1], scale=SWA_SCALE,
                                             accum_out=stat(s, TOTAL)[:, hd:hd + 1])
                    nc.scalar.activation(stat(s, SINKE), stat(s, SINKN), ACT.Exp).then_inc(s_exp, 1)
                    if n == 0 and gh + 1 < 4:
                        if gh >= 1:
                            act.wait_ge(s_qk, 4 * gh)
                        split_queries_hi(gh + 1)
                    if n == 3 and gh + 2 < 4:
                        load_band(gh + 2)

            for e in range(2):
                rows = slice(64 * e, 64 * e + 64)
                act.wait_ge(made_m, 4)
                act.wait_ge(r_done, 1)
                copy_hi(krp[0][rows, e, :], t_a[rows, :])
            for p in range(PAIRS):
                def copy_from(waited, value, dst, b):
                    act.wait_ge(waited, value)
                    copy_hi(dst, b)

                if p:
                    act.wait_ge(m_pv, 2 * p)
                qp, proj = Q_MLA + 2 * p, PROJ * p
                copy_from(m_proj, proj + 1, kn[0][:, 0, :], bank[0])
                copy_from(m_proj, proj + 2, kn[0][:, 1, :], bank[1])
                copy_from(m_proj, proj + 3, vn[0][:, 0:2, :], bank[2].rearrange("p (t n) -> p t n", t=2))
                copy_from(used, qp + 1, vn[0][:, 2:4, :], bank[3].rearrange("p (t n) -> p t n", t=2))
                split_hi(qp + 2, qp % 2)
                copy_from(m_proj, proj + 5, qn[0][:, 0, :], bank[4])
                copy_from(r_done, p + 2, qr[0][:, :], t_a[:, :])
                copy_from(used, qp + 2, qn[0][:, 1, :], bank[5])

                def exponentials(h):
                    act.wait_ge(m_neg, h + 1)
                    for i in range(TB):
                        blk = mp[h % 2][:, i, 0:P * (i + 1)]
                        nc.scalar.activation(blk, blk, ACT.Exp, bias=stat(h, NEGM)[:, i:i + 1],
                                             scale=MLA_SCALE, accum_out=stat(h, TOTAL)[:, i:i + 1]
                                             ).then_inc(m_exp, 1)

                def transposed_hi(h):
                    if h >= 2:
                        act.wait_ge(m_pv, h - 1)
                    for i, (o, w) in enumerate(PT_PARTS):
                        act.wait_ge(m_t, 3 * h + i + 1)
                        nc.scalar.activation(mpt[h % 2][0][:, o:o + w], bank[4 + i][:, 0:w],
                                             ACT.Copy).then_inc(m_hi, 1)

                def head_out(h):
                    act.wait_ge(m_pv, h + 1)
                    nc.scalar.activation(mix_m[:, h, :], bank[7], ACT.Copy).then_inc(m_out, 1)

                exponentials(2 * p)
                transposed_hi(2 * p)
                exponentials(2 * p + 1)
                head_out(2 * p)
                transposed_hi(2 * p + 1)
                head_out(2 * p + 1)
                split_hi(qp + 3, (qp + 1) % 2)

            act.dma_start(gpost[:, :], g_mix_post.broadcast_to([P, D])).then_inc(gpost_in, 16)
            act.wait_ge(s_out, UNITS)
            act.wait_ge(m_out, MLA_HEADS)
            for c in MIX_ORDER:
                copy_hi(mixt[0][:, c, :], mix_chunk(c))
            for i in range(16):
                q = Q_OUT + i
                if i % 4 == 3:
                    for t in range(TB):
                        if t < TB - 1:
                            act.wait_ge(o_bank, 3 * (i // 4) + t + 1)
                        else:
                            act.wait_ge(used, q + 1)
                        if i > 3 or t:
                            act.wait_ge(o_sq, 4 * (i // 4) + t)
                        nc.scalar.activation(junk4[:, 0:512], bank[4 * (i // 4 % 2) + t], ACT.Square,
                                             accum_out=ss4[:, t, i // 4:i // 4 + 1]).then_inc(o_sq, 1)
                        if i == 15:
                            act.wait_ge(mean_done, 3 + t + 1)
                            nc.scalar.activation(root[:, t:t + 1], mean[:, t:t + 1], ACT.Sqrt).then_inc(root_done, 1)
                            act.wait_ge(o_taken, O_BASE - TB + t + 1)
                            act.wait_ge(rstd_ready, t + 1)
                            for n in (2, 3):
                                residual_times(mixn, t, slice(512 * n, 512 * n + 512)).then_inc(scaled, 1)
                if i < 15:
                    split_hi(q + 2, q % 2)
            for c in range(KD):
                if c == 8:
                    split_hi(Q_FFN + 1, (Q_FFN + 1) % 2)
                act.wait_ge(tr, KD + c + 1)
                copy_hi(act_hi[:, c, :], chunk_bank(c), gffn[:, c:c + 1])
            act.wait_ge(x1_ready, 2 * TB)
            act.wait_ge(x1_pool, 2 * TB)
            act.wait_ge(o_sq, 16)
            token_squares(x1, junk4)
            act.wait_ge(mean_done, 8)
            nc.scalar.activation(root[:, :], mean[:, :], ACT.Sqrt).then_inc(root_done, 1)
            split_hi(Q_FFN + 2, Q_FFN % 2)

            def feed(b):
                for j in range(PER_BLOCK):
                    q = b * PER_BLOCK + (Q_FFN + j)
                    slot = (Q_FFN + j) % 2
                    i = j // 2
                    if j < 8 and j % 2 == 0:
                        act.wait_ge(gated, b * 4 + (i + 1))
                        nc.scalar.activation(sil[:, :], sil[:, :], ACT.Silu).then_inc(silu_done, 1)
                    elif j < 8:
                        act.wait_ge(g_done, b * 4 + (i + 1))
                        nc.scalar.activation(gt[0][:, i, :], gf[:, :], ACT.Copy).then_inc(g_hi, 1)
                    if isinstance(b, int) and (q == Q_FFN or q + 2 >= Q_END):
                        pass
                    else:
                        split_hi(q + 2, slot)
                    if isinstance(b, int) and b == BLOCKS - 1 and j == PER_BLOCK - 2:
                        nc.scalar.activation(root[:, 0:1], mean[:, 0:1], ACT.Sqrt)

            feed(0)
            with act.Fori(1, BLOCKS - 1) as b:
                feed(b)
            feed(BLOCKS - 1)
            for i in range(16):
                act.wait_ge(o_taken, O_BASE + 16 * (BLOCKS - 1) + i + 1)
                act.wait_ge(o_sq, 16 + i)
                cb, t = i // 4, i % 4
                nc.scalar.activation(junk6[:, :], acc[:, t, 512 * cb:512 * cb + 512], ACT.Square,
                                     accum_out=ss4[:, t, cb:cb + 1]).then_inc(o_sq, 1)
                if cb == 3:
                    act.wait_ge(mean_done, 8 + t + 1)
                    nc.scalar.activation(root[:, t:t + 1], mean[:, t:t + 1], ACT.Sqrt).then_inc(root_done, 1)
                    act.wait_ge(gained, 8 + 2 * t + 2)
                    act.wait_ge(rstd_ready, TB + t + 1)
                    residual_times(acc, t, shared(t)).then_inc(scaled, 1)

        @block.vector
        def _(dve):
            chain = [0]

            def link(ins):
                chain[0] += 1
                ins.then_inc(link_s, 1)
                dve.wait_ge(link_s, chain[0])

            def sub_lo(dst, src, hi):
                lows[0] += 1
                dve.wait_ge(act_h, lows[0])
                nc.vector.tensor_tensor(dst, src, f(hi), ALU.subtract).then_inc(act_l, 1)

            def scaled_lo(dst, src, g, hi):
                lows[0] += 1
                dve.wait_ge(act_h, lows[0])
                nc.vector.scalar_tensor_tensor(out=dst, in0=src, scalar=g, in1=f(hi), op0=ALU.mult,
                                               op1=ALU.subtract).then_inc(act_l, 1)

            lows = [0]

            def inverse_root(v, r, y, a, c, res):
                link(nc.vector.reciprocal(y, r))
                link(nc.vector.tensor_tensor(a, v, y, ALU.mult))
                link(nc.vector.tensor_tensor(a, a, y, ALU.mult))
                link(nc.vector.tensor_scalar(c, a, -0.5, 1.5, ALU.mult, ALU.add))
                return nc.vector.tensor_tensor(res, y, c, ALU.mult)

            dve.wait_ge(gains_mm, 1)
            nc.vector.tensor_copy(gpre, bank[7][:, 0:KD]).then_inc(gain_cols, 1)

            def norm_column(col, count):
                dve.wait_ge(sumsq_x, TB * count)
                nc.vector.tensor_scalar(mean, ssum, 1.0 / D, EPS, ALU.mult, ALU.add).then_inc(mean_done, 1)
                dve.wait_ge(root_done, (1, 8)[count - 1])
                link(inverse_root(mean, root, y0, yy, cc_, rstd))
                for t in range(TB):
                    last = nc.vector.tensor_scalar(col[:, t, :], ones[:, :], rstd[:, t:t + 1], None, ALU.mult)
                last.then_inc(rcol_ready, 1)

            def take_norm_row(row, count):
                dve.wait_ge(rrow_mm, count)
                nc.vector.tensor_copy(row[:, :], bank[7]).then_inc(rrow_ready, 1)
                dve.wait_ge(rrow_ready, count)

            split_lo(0, 0)
            for c in range(KD):
                if c == 12:
                    split_lo(1, 1)
                scaled_lo(act_lo0[:, c, :], chunk_bank(c), gpre[:, c:c + 1], act_hi0[:, c, :])
            dve.wait_ge(cols_in, 32)
            link(nc.vector.tensor_scalar(sink8, sink8, 1.0 / SWA_SCALE, None, ALU.mult))

            dve.wait_ge(gains_mm, 2)
            nc.vector.tensor_copy(gains[:, KD:], bank[7][:, KD:N_GAIN]).then_inc(gain_cols, 1)
            dve.wait_ge(bias_mm, 1)
            nc.vector.tensor_scalar(brow[:, :], bank[6][0:16, 0:BIAS_W], 1.0 / SWA_SCALE, None,
                                    ALU.mult).then_inc(brow_ready, 1)

            norm_column(rcol0, 1)
            split_lo(2, 0)
            take_norm_row(rrow0, 1)

            def turns():
                dve.wait_ge(pos_in, 16)
                link(nc.vector.tensor_copy(ang[:, :], pos_i[:, :]))
                link(nc.vector.tensor_scalar(ang[:, :], ang[:, :], invf, None, ALU.mult))
                link(nc.vector.tensor_scalar(kk[:, :], ang[:, :], 1.0 / TWO_PI, MAGIC, ALU.mult, ALU.add))
                link(nc.vector.tensor_scalar(kk[:, :], kk[:, :], MAGIC, None, ALU.subtract))
                link(nc.vector.tensor_scalar(kh[:, :], kk[:, :], 1.0 / 2048, MAGIC, ALU.mult, ALU.add))
                link(nc.vector.tensor_scalar(kh[:, :], kh[:, :], MAGIC, None, ALU.subtract))
                link(nc.vector.scalar_tensor_tensor(out=kk[:, :], in0=kh[:, :], scalar=-2048.0, in1=kk[:, :],
                                                    op0=ALU.mult, op1=ALU.add))

            def angles():
                for c in two_pi_pieces():
                    link(nc.vector.scalar_tensor_tensor(out=ang[:, :], in0=kh[:, :], scalar=-2048.0 * c,
                                                        in1=ang[:, :], op0=ALU.mult, op1=ALU.add))
                    link(nc.vector.scalar_tensor_tensor(out=ang[:, :], in0=kk[:, :], scalar=-c, in1=ang[:, :],
                                                        op0=ALU.mult, op1=ALU.add))
                nc.vector.tensor_scalar(ang[:, :], ang[:, :], 3.1415925, -3.1415925, ALU.min,
                                        ALU.max).then_inc(angle_done, 1)

            def latent_norm(n):
                dve.wait_ge(sumsq_c, KL * (n + 1))
                nc.vector.tensor_scalar(w_ms[:, :], bank[2 + n], 1.0 / LORA, EPS, ALU.mult,
                                        ALU.add).then_inc(mean_done, 1)
                dve.wait_ge(root_done, n + 2)
                link(inverse_root(w_ms[:, :], w_y[:, :], w_y[:, :], w_a[:, :], w_a[:, :], w_y[:, :]))
                for i in range(KL):
                    nc.vector.scalar_tensor_tensor(out=craw[n][:, i, :], in0=craw[n][:, i, :],
                                                   scalar=(gckv, gcq)[n][:, i:i + 1], in1=w_y[:, :],
                                                   op0=ALU.mult, op1=ALU.mult).then_inc(normed, 1)
                for i in range(KL):
                    sub_lo((ckv, cq)[n][1][:, i, :], craw[n][:, i, :], (ckv, cq)[n][0][:, i, :])

            def split_queries_lo(gh):
                dve.wait_ge(q_hi, gh + 1)
                nc.vector.tensor_tensor(qs[gh % 2][1][:, :, :], sq[:, 2 * gh:2 * gh + 2, :],
                                        f(qs[gh % 2][0][:, :, :]), ALU.subtract).then_inc(q_lo, 1)

            for q in range(N_IN):
                what, j, _ = IN_PANELS[q]
                b = in_bank(q)

                def take(dst, rows=slice(0, P)):
                    return nc.vector.tensor_tensor(dst, b[rows, :], rrow0[rows, :], ALU.mult)

                dve.wait_ge(used, q + 1)
                if what in ("ckv", "cq"):
                    take(craw[q // KL][:, j, :]).then_inc(taken, 1)
                elif what == "kr":
                    take(kraw[0:64, :], slice(0, 64))
                    take(kraw[64:128, :], slice(0, 64)).then_inc(taken, 1)
                elif what == "sk":
                    for i in range(4):
                        g, e = i // 2, i % 2
                        last = take(skd[64 * e:64 * e + 64, g, :], slice(64 * g, 64 * g + 64))
                    last.then_inc(taken, 1)
                elif what == "sv":
                    take(svt[:, :]).then_inc(taken, 1)
                else:
                    take(sq[:, j, :]).then_inc(taken, 1)
                if q:
                    split_lo(q + 2, q % 2)
                if q == 1:
                    turns()
                if q == 2:
                    angles()
                if q == 3:
                    dve.wait_ge(sines, 2)
                    link(nc.vector.tensor_tensor(kk[:, :], kk[:, :], kk[:, :], ALU.mult))
                    link(nc.vector.tensor_scalar(cos_t[:, :], kk[:, :], -2.0, 1.0, ALU.mult, ALU.add))
                if q in (KL, 2 * KL):
                    latent_norm(q // KL - 1)
                if q == N_IN - 4:
                    split_queries_lo(0)
                if what == "sk":
                    for i in range(4):
                        g, e = i // 2, i % 2
                        rows = slice(64 * e, 64 * e + 64)
                        sub_lo(kpad[1][rows, g, e, :], skd[rows, g, :], kpad[0][rows, g, e, :])
                if q == N_IN - 8:
                    sub_lo(vpad[1][:, :, :, 64:128], bank[4].rearrange("p (b g d) -> p b g d", b=TB, g=2),
                           vpad[0][:, :, :, 64:128])

            for s in range(UNITS + 2):
                def reciprocals():
                    if 1 <= s < UNITS + 1:
                        u = s - 1
                        dve.wait_ge(s_exp, u + 1)
                        link(nc.vector.tensor_tensor(stat(u, MAXI), stat(u, TOTAL), stat(u, SINKE), ALU.add))
                        nc.vector.reciprocal(stat(u, RECI), stat(u, MAXI)).then_inc(s_reci, 1)

                if s == UNITS:
                    reciprocals()
                if s < UNITS:
                    gh, _, n, lo = unit(s)
                    dve.wait_ge(s_qk, s + 1)
                    if n == 0:
                        dve.wait_ge(band_in[gh % 2], 16 * (gh // 2 + 1))
                    if s >= 3:
                        dve.wait_ge(s_t, halves(s - 3)[-1][1] + 1)
                    for hd in range(4):
                        if hd == 2:
                            reciprocals()
                        scores = bank[(s + 1) % 2 * 2 + hd // 2].rearrange("p (e k) -> p e k", e=2)[:, hd % 2, lo:256]
                        last = nc.vector.tensor_tensor_reduce(
                            sp[s % 3][:, hd, lo:256], scores, bias_t[gh % 2][:, hd, lo:256], 1.0, -3e38,
                            ALU.add, ALU.max, stat(s, MAXI)[:, hd:hd + 1])
                    link(last)
                    link(nc.vector.tensor_tensor(stat(s, MAXI), stat(s, MAXI), sink8[:, 4 * gh:4 * gh + 4],
                                                 ALU.max))
                    link(nc.vector.tensor_scalar(stat(s, NEGM), stat(s, MAXI), -SWA_SCALE, None, ALU.mult))
                    nc.vector.scalar_tensor_tensor(out=stat(s, SINKN), in0=sink8[:, 4 * gh:4 * gh + 4],
                                                   scalar=SWA_SCALE, in1=stat(s, NEGM), op0=ALU.mult,
                                                   op1=ALU.add).then_inc(s_max, 1)
                if s >= 2:
                    u = s - 2
                    for kb, h in halves(u):
                        dve.wait_ge(s_hi, h + 1)
                        nc.vector.tensor_tensor(spt[u % 2][1][:, kb, :], half_bank(h),
                                                f(spt[u % 2][0][:, kb, :]), ALU.subtract).then_inc(s_lo, 1)
                if s < UNITS and s % 4 == 0 and s // 4 + 1 < 4:
                    split_queries_lo(s // 4 + 1)

            def rotate(src, n):
                link(nc.vector.tensor_tensor(t_a[:, :], src, cos_t[:, :], ALU.mult))
                dve.wait_ge(r_perm, n + 1)
                link(nc.vector.tensor_tensor(t_b[:, :], bank[7], sin_t[:, :], ALU.mult))
                nc.vector.tensor_tensor(t_a[:, :], t_a[:, :], t_b[:, :], ALU.add).then_inc(r_done, 1)

            dve.wait_ge(s_pv, UNITS)
            rotate(kraw[:, :], 0)
            for e in range(2):
                rows = slice(64 * e, 64 * e + 64)
                sub_lo(krp[1][rows, e, :], t_a[rows, :], krp[0][rows, e, :])
            for p in range(PAIRS):
                sub_lo(kn[1][:, 0, :], bank[0], kn[0][:, 0, :])
                sub_lo(kn[1][:, 1, :], bank[1], kn[0][:, 1, :])
                for i in range(2):
                    sub_lo(vn[1][:, 2 * i:2 * i + 2, :], bank[2 + i].rearrange("p (t n) -> p t n", t=2),
                           vn[0][:, 2 * i:2 * i + 2, :])
                split_lo(Q_MLA + 2 * p + 2, Q_MLA % 2)
                dve.wait_ge(m_proj, PROJ * p + 4)
                nc.vector.tensor_copy(t_sb[:, :], bank[6]).then_inc(r_in, 1)
                sub_lo(qn[1][:, 0, :], bank[4], qn[0][:, 0, :])
                dve.wait_ge(r_in, p + 1)
                rotate(t_sb[:, :], p + 1)
                sub_lo(qr[1][:, :], t_a[:, :], qr[0][:, :])
                sub_lo(qn[1][:, 1, :], bank[5], qn[0][:, 1, :])

                def maxima(h):
                    if h == 0:
                        dve.wait_ge(made_m, 6)
                    if h >= 2:
                        dve.wait_ge(m_t, 3 * (h - 1))
                    for i in range(TB):
                        w = P * (i + 1)
                        dve.wait_ge(m_qk, 4 * h + i + 1)
                        last = nc.vector.tensor_tensor_reduce(
                            mp[h % 2][:, i, 0:w], bank[i][:, 0:w], tri[:, 384 - P * i:512], 1.0, -3e38,
                            ALU.add, ALU.max, stat(h, MAXI)[:, i:i + 1])
                        last.then_inc(m_max, 1)
                    dve.wait_ge(m_max, 4 * h + 4)
                    nc.vector.tensor_scalar(stat(h, NEGM), stat(h, MAXI), -MLA_SCALE, None,
                                            ALU.mult).then_inc(m_neg, 1)

                def probabilities(h):
                    dve.wait_ge(m_exp, 4 * h + 4)
                    link(nc.vector.reciprocal(stat(h, RECI), stat(h, TOTAL)))
                    for i in range(TB):
                        blk = mp[h % 2][:, i, 0:P * (i + 1)]
                        nc.vector.tensor_scalar(blk, blk, stat(h, RECI)[:, i:i + 1], None,
                                                ALU.mult).then_inc(m_norm, 1)

                def transposed_lo(h):
                    for i, (o, w) in enumerate(PT_PARTS):
                        dve.wait_ge(m_hi, 3 * h + i + 1)
                        nc.vector.tensor_tensor(mpt[h % 2][1][:, o:o + w], bank[4 + i][:, 0:w],
                                                f(mpt[h % 2][0][:, o:o + w]), ALU.subtract).then_inc(m_lo, 1)

                maxima(2 * p)
                probabilities(2 * p)
                maxima(2 * p + 1)
                transposed_lo(2 * p)
                probabilities(2 * p + 1)
                transposed_lo(2 * p + 1)
                split_lo(Q_MLA + 2 * p + 3, (Q_MLA + 1) % 2)

            def token_rstd(t, squares_before, norms_before, meanwhile):
                c = slice(t, t + 1)
                dve.wait_ge(o_sq, squares_before + t + 1)
                link(nc.vector.tensor_reduce(ssum[:, c], ss4[:, t, :], AX.X, ALU.add))
                nc.vector.tensor_scalar(mean[:, c], ssum[:, c], 1.0 / D, EPS, ALU.mult,
                                        ALU.add).then_inc(mean_done, 1)
                meanwhile()
                dve.wait_ge(root_done, norms_before + t + 1)
                inverse_root(mean[:, c], root[:, c], y0[:, c], yy[:, c], cc_[:, c],
                             rstd[:, c]).then_inc(rstd_ready, 1)
                dve.wait_ge(rstd_ready, (TB if norms_before > 3 else 0) + t + 1)

            for c in MIX_ORDER:
                sub_lo(mixt[1][:, c, :], mix_chunk(c), mixt[0][:, c, :])
            for i in range(16):
                q = Q_OUT + i
                if i == 3:
                    dve.wait_ge(gpost_in, 16)
                    dve.wait_ge(x_again, 16 * TB)
                if i % 4 == 3:
                    cb = i // 4
                    for t in range(TB):
                        def take():
                            nc.vector.tensor_tensor(mixn[:, t, 512 * cb:512 * cb + 512], bank[4 * (cb % 2) + t],
                                                    gpost[:, 512 * cb:512 * cb + 512], ALU.mult
                                                    ).then_inc(o_taken, 1)

                        dve.wait_ge(o_sq, 4 * cb + t + 1)
                        if cb < 3:
                            take()
                        else:
                            token_rstd(t, 12, 3, take)
                            dve.wait_ge(o_taken, O_BASE - TB + t + 1)
                            residual(mixn, t, slice(0, 512)).then_inc(x1_ready, 1)
                if i < 15:
                    split_lo(q + 2, q % 2)
            for t in range(TB):
                residual(mixn, t, slice(512, 1024)).then_inc(x1_ready, 1)

            for c in range(KD):
                if c == 8:
                    split_lo(Q_FFN + 1, (Q_FFN + 1) % 2)
                scaled_lo(act_lo[:, c, :], chunk_bank(c), gffn[:, c:c + 1], act_hi[:, c, :])
            norm_column(rcol, 2)
            split_lo(Q_FFN + 2, Q_FFN % 2)
            take_norm_row(rrow, 2)

            dve.wait_ge(acc_zero, 1)

            def times_gain(cb, t):
                dve.wait_ge(o_sq, 16 + 4 * cb + t + 1)
                a = acc[:, t, 512 * cb:512 * cb + 512]
                nc.vector.tensor_tensor(a, a, raw[Q_END % 2][:, 512 * cb:512 * cb + 512],
                                        ALU.mult).then_inc(gained, 1)

            def feed(b):
                final = isinstance(b, int) and b == BLOCKS - 1
                for j in range(PER_BLOCK):
                    q = b * PER_BLOCK + (Q_FFN + j)
                    slot = (Q_FFN + j) % 2
                    i = j // 2
                    if j < 8 and j % 2 == 0:
                        dve.wait_ge(used, q + 1)
                        nc.vector.tensor_tensor(sil[:, :], bank[i % 2], rrow[:, :], ALU.mult).then_inc(gated, 1)
                    if j < 8 and j % 2:
                        dve.wait_ge(silu_done, b * 4 + (i + 1))
                        nc.vector.tensor_tensor(sil[:, :], sil[:, :], rrow[:, :], ALU.mult).then_inc(sil_normed, 1)
                        dve.wait_ge(sil_normed, b * 4 + (i + 1))
                        dve.wait_ge(used, q + 1)
                        nc.vector.tensor_tensor(gf[:, :], bank[2 + i % 2], sil[:, :], ALU.mult).then_inc(g_done, 1)
                        dve.wait_ge(g_hi, b * 4 + (i + 1))
                        nc.vector.tensor_tensor(gt[1][:, i, :], gf[:, :], f(gt[0][:, i, :]),
                                                ALU.subtract).then_inc(g_lo, 1)
                    if j >= 8:
                        cb = j - 8
                        for t in range(TB):
                            if t < TB - 1:
                                dve.wait_ge(d_bank, b * 12 + (3 * cb + t + 1))
                            else:
                                dve.wait_ge(used, q + 1)
                            a = acc[:, t, 512 * cb:512 * cb + 512]
                            nc.vector.tensor_tensor(a, a, bank[(4, 0)[cb % 2] + t], ALU.add).then_inc(o_taken, 1)
                            if final and cb == 2:
                                if t == 0:
                                    dve.wait_ge(raw_in[Q_END % 2], (Q_END - Q_END % 2) * 8 + 16)
                                times_gain(0, t)
                                times_gain(1, t)
                            if final and cb == 3:
                                times_gain(2, t)
                                token_rstd(t, 28, 8, lambda: times_gain(3, t))
                                dve.wait_ge(gained, 8 + 2 * t + 2)
                                residual(acc, t, slice(shared(t).stop, D)).then_inc(y_ready, 1)
                    if not isinstance(b, int) or Q_FFN < q < Q_END - 2:
                        split_lo(q + 2, slot)

            feed(0)
            with dve.Fori(1, BLOCKS - 1) as b:
                feed(b)
            feed(BLOCKS - 1)

        @block.tensor
        def _(pe):
            pe.wait_ge(made, 7)
            pe.wait_ge(gpre_in, 16)
            nc.tensor.transpose(bank[7][:, 0:KD], gpre_rows[:, :], ident[0:KD, 0:KD]).then_inc(gains_mm, 1)

            def transposed_and_multiplied(src, before, wait_src, w_panel, operand):
                hi, lo = k16(whi[w_panel % 2]), k16(wlo[w_panel % 2])

                def transpose_chunk(c):
                    wait_src(c)
                    if c >= CHUNK_BANKS:
                        pe.wait_ge(act_l, before + c - CHUNK_BANKS + 1)
                    for t in range(TB):
                        last = nc.tensor.transpose(chunk_bank(c)[:, P * t:P * t + P],
                                                   src[:, t, P * c:P * c + P], ident[:, :])
                    last.then_inc(tr, 1)

                for c in range(AHEAD):
                    transpose_chunk(c)
                for k in range(KD):
                    if k + AHEAD < KD:
                        transpose_chunk(k + AHEAD)
                    if k == 0:
                        pe.wait_ge(lo_ready, w_panel + 1)
                    pe.wait_ge(act_l, before + k + 1)
                    last = three(bank[0], (hi[:, k, :], lo[:, k, :]), (operand[0][:, k, :], operand[1][:, k, :]),
                                 k == 0, k == KD - 1)
                last.then_inc(used, 1)

            def norm_row(col, count):
                pe.wait_ge(rcol_ready, count)
                for t in range(TB):
                    last = nc.tensor.transpose(bank[7][:, P * t:P * t + P], col[:, t, :], ident[:, :])
                last.then_inc(rrow_mm, 1)

            def x_ready(c):
                if c % 4 == 0:
                    pe.wait_ge(x_in[c // 4], 16)
            transposed_and_multiplied(xin, 0, x_ready, 0, (act_hi0, act_lo0))
            pe.wait_ge(gain_cols, 1)
            pe.wait_ge(rows_in, 48)
            nc.tensor.transpose(bank[7][:, KD:N_GAIN], gain_rows[:, :],
                                ident[0:N_GAIN - KD, 0:N_GAIN - KD]).then_inc(gains_mm, 1)
            pe.wait_ge(bias_src_in, 32)
            nc.tensor.matmul(bank[6][0:16, 0:BIAS_W], relaug[:, :], bsel[:, :], start=True,
                             stop=True).then_inc(bias_mm, 1)

            def latent_sum(q):
                pe.wait_ge(squares, q + 1)
                nc.tensor.matmul(bank[2 + q // KL], ones[:, :], sqt[:, :], start=(q % KL == 0),
                                 stop=(q % KL == KL - 1)).then_inc(sumsq_c, 1)

            for q in range(1, N_IN):
                pe.wait_ge(lo_ready, q + 1)
                if q >= 3:
                    pe.wait_ge(taken, q - 2)
                hi, lo = k16(whi[q % 2]), k16(wlo[q % 2])
                for k in range(KD):
                    last = three(in_bank(q), (hi[:, k, :], lo[:, k, :]), (act_hi0[:, k, :], act_lo0[:, k, :]),
                                 k == 0, k == KD - 1)
                last.then_inc(used, 1)
                if q == 1:
                    pe.wait_ge(gain_cols, 2)
                    norm_row(rcol0, 1)
                if q == 2:
                    latent_sum(0)
                if 2 <= q <= 2 * KL:
                    latent_sum(q - 1)
                if q == N_IN - 8:
                    pe.wait_ge(taken, N_IN - 8)
                    for t in range(TB):
                        last = nc.tensor.transpose(bank[4][:, P * t:P * t + P], svt[:, P * t:P * t + P], ident[:, :])
                    last.then_inc(sv_t, 1)

            for s in range(UNITS + 3):
                if s < UNITS:
                    gh, g, n, lo = unit(s)
                    if n == 0:
                        pe.wait_ge(q_lo, gh + 1)
                    if s == 0:
                        pe.wait_ge(mean_done, 3)
                        pe.wait_ge(act_l, N_SV)
                    if s == 1:
                        pe.wait_ge(taken, N_IN)
                    if s >= 2:
                        pe.wait_ge(s_max, s - 1)
                    keys = slice(P * n - P + lo, P * n + P)
                    for cc in range(2):
                        dst = bank[(s + 1) % 2 * 2 + cc].rearrange("p (e k) -> p e k", e=2)[:, :, lo:256]
                        last = three(dst, [qs[gh % 2][i][:, cc, P * n:P * n + P] for i in range(2)],
                                     [kpad[i][:, g, :, keys] for i in range(2)], True, True)
                    last.then_inc(s_qk, 1)
                if 2 <= s < UNITS + 2:
                    u = s - 2
                    pe.wait_ge(s_norm, u + 1)
                    for kb, h in halves(u):
                        if h >= 3:
                            pe.wait_ge(s_lo, h - 2)
                        for cc in range(2):
                            for e in range(2):
                                o = P * (2 * e + cc)
                                last = nc.tensor.transpose(half_bank(h)[:, o:o + P],
                                                           sp[u % 3][:, 2 * cc + e, P * kb:P * kb + P], ident[:, :])
                        last.then_inc(s_t, 1)
                if s >= 3:
                    u = s - 3
                    gh, g, n, lo = unit(u)
                    if u >= 1:
                        pe.wait_ge(s_out, u)
                    parts = [(kb, e, h) for kb, h in halves(u) for e in range(2)]
                    for m, (kb, e, h) in enumerate(parts):
                        pe.wait_ge(s_lo, h + 1)
                        c0 = 64 - 64 * e
                        last = three(bank[7][:, 0:256],
                                     [vpad[i][:, n - 1 + kb, g, c0:c0 + P] for i in range(2)],
                                     [spt[u % 2][i][:, kb, 256 * e:256 * e + 256] for i in range(2)],
                                     m == 0, m == len(parts) - 1)
                    last.then_inc(s_pv, 1)

            def permute(src, n):
                nc.tensor.matmul(bank[7], rot[:, :], src, start=True, stop=True).then_inc(r_perm, 1)

            pe.wait_ge(s_out, UNITS)
            permute(kraw[:, :], 0)
            for p in range(PAIRS):
                q = Q_MLA + 2 * p
                hi, lo = k4(whi[q % 2]), k4(wlo[q % 2])
                pe.wait_ge(lo_ready, q + 1)
                if p == 0:
                    pe.wait_ge(s_max, UNITS)
                else:
                    pe.wait_ge(m_max, 4 * 2 * p)
                for hh in range(2):
                    for k in range(KL):
                        c0 = 256 * hh
                        last = three(bank[hh], (hi[:, k, c0:c0 + P], lo[:, k, c0:c0 + P]),
                                     (ckv[0][:, k, :], ckv[1][:, k, :]), k == 0, k == KL - 1)
                    last.then_inc(m_proj, 1)
                for t in range(TB):
                    for k in range(KL):
                        v = [w[:, k, :].rearrange("p (h n) -> p h n", h=2)[:, :, P:256] for w in (hi, lo)]
                        dst = bank[2 + t // 2][:, 256 * (t % 2):256 * (t % 2) + 256]
                        last = three(dst.rearrange("p (h n) -> p h n", h=2),
                                     [ckv[i][:, k, P * t:P * t + P] for i in range(2)], v, k == 0, k == KL - 1)
                    if t == 1:
                        last.then_inc(m_proj, 1)
                last.then_inc(used, 1)
                q += 1
                hi, lo = k4(whi[q % 2], 384), k4(wlo[q % 2], 384)
                pe.wait_ge(lo_ready, q + 1)
                if p == 0:
                    pe.wait_ge(s_lo, N_HALVES)
                else:
                    pe.wait_ge(m_lo, 3 * 2 * p)
                for k in range(KL):
                    r = [w[:, k, 2 * NOPE:384] for w in (hi, lo)]
                    last = three(bank[6], r, (cq[0][:, k, :], cq[1][:, k, :]), k == 0, k == KL - 1)
                last.then_inc(m_proj, 1)
                for hh in range(2):
                    for k in range(KL):
                        c0 = NOPE * hh
                        last = three(bank[4 + hh], (hi[:, k, c0:c0 + P], lo[:, k, c0:c0 + P]),
                                     (cq[0][:, k, :], cq[1][:, k, :]), k == 0, k == KL - 1)
                    if hh == 0:
                        last.then_inc(m_proj, 1)
                last.then_inc(used, 1)
                pe.wait_ge(r_in, p + 1)
                pe.wait_ge(r_done, p + 1)
                if p:
                    pe.wait_ge(m_out, 2 * p)
                permute(t_sb[:, :], p + 1)

                def scores(h):
                    hh = h % 2
                    done = N_KR + PER_PAIR * p
                    pe.wait_ge(act_l, done + (5 if hh == 0 else 7))
                    for i in range(TB):
                        if h:
                            pe.wait_ge(m_max, 4 * (h - 1) + i + 1)
                        w = max(256, P * (i + 1))
                        three(bank[i][:, 0:w], [qn[m][:, hh, P * i:P * i + P] for m in range(2)],
                              [kn[m][:, hh, 0:w] for m in range(2)], True, False)
                    pe.wait_ge(act_l, done + 6 + hh)
                    for i in range(TB):
                        w = max(256, P * (i + 1))
                        three(bank[i][:, 0:w], [qr[m][:, P * i:P * i + P] for m in range(2)],
                              [krp[m][:, hh, 0:w] for m in range(2)], False, True).then_inc(m_qk, 1)

                def transposes(h):
                    pe.wait_ge(m_norm, 4 * h + 4)
                    for n, blocks in enumerate((((0, 0), (0, 1), (0, 2), (0, 3)), ((1, 1), (1, 2), (1, 3)),
                                                ((2, 2), (2, 3), (3, 2), (3, 3)))):
                        if h:
                            pe.wait_ge(m_lo, 3 * (h - 1) + n + 1)
                        for o, (j, i) in enumerate(blocks):
                            last = nc.tensor.transpose(bank[4 + n][:, P * o:P * o + P],
                                                       mp[h % 2][:, i, P * j:P * j + P], ident[:, :])
                        last.then_inc(m_t, 1)

                def values(h):
                    hh = h % 2
                    if h:
                        pe.wait_ge(m_out, h)
                    for j, (o, w, n) in enumerate(((0, 512, 1), (512, 384, 2), (896, 256, 3), (1152, 256, 3))):
                        pe.wait_ge(m_lo, 3 * h + n)
                        last = three(bank[7][:, 512 - w:512], [vn[m][:, j, P * hh:P * hh + P] for m in range(2)],
                                     [mpt[h % 2][m][:, o:o + w] for m in range(2)], j == 0, j == TB - 1)
                    last.then_inc(m_pv, 1)

                scores(2 * p)
                scores(2 * p + 1)
                transposes(2 * p)
                values(2 * p)
                transposes(2 * p + 1)
                values(2 * p + 1)

            for i in range(16):
                q = Q_OUT + i
                cb, kg = i // 4, KG_ORDER[i % 4]
                hi, lo = k4(whi[q % 2]), k4(wlo[q % 2])
                pe.wait_ge(lo_ready, q + 1)
                if i == 0:
                    pe.wait_ge(m_max, 4 * MLA_HEADS)
                if i == 4:
                    pe.wait_ge(m_lo, 3 * MLA_HEADS)
                    pe.wait_ge(m_out, MLA_HEADS)
                order = [(k, t) for k in range(4) for t in range(TB)]
                if i % 4 == 3:
                    order = [(k, t) for t in range(TB) for k in range(4)]
                for k, t in order:
                    if i < 4 and t == 0:
                        pe.wait_ge(act_l, N_PAIRS + 4 * i + k + 1)
                    if i % 4 == 0 and k == 0 and cb >= 2:
                        pe.wait_ge(o_taken, 4 * (cb - 2) + t + 1)
                    c = 4 * kg + k
                    last = three(bank[4 * (cb % 2) + t], [mixt[m][:, c, P * t:P * t + P] for m in range(2)],
                                 (hi[:, k, :], lo[:, k, :]), i % 4 == 0 and k == 0, i % 4 == 3 and k == 3)
                    if i % 4 == 3 and k == 3 and t < TB - 1:
                        last.then_inc(o_bank, 1)
                last.then_inc(used, 1)

            def x1_chunk_ready(c):
                if c % 4 == 0 and c < 8:
                    pe.wait_ge(x1_ready, TB * (c // 4 + 1))
                if c >= 8 and c % 4 == 0:
                    pe.wait_ge(x1_pool, 2 * TB)
                if c == 0:
                    pe.wait_ge(o_taken, O_BASE)

            transposed_and_multiplied(x1, N_MIX, x1_chunk_ready, Q_FFN, (act_hi, act_lo))

            def feed(b):
                first = isinstance(b, int) and b == 0
                for j in range(1 if first else 0, PER_BLOCK):
                    q = b * PER_BLOCK + (Q_FFN + j)
                    slot = (Q_FFN + j) % 2
                    i = j // 2
                    pe.wait_ge(lo_ready, q + 1)
                    if j < 8:
                        dst = bank[2 * (j % 2) + i % 2]
                        if j < 4 and not first:
                            pe.wait_ge(o_taken, b * 16 + (O_BASE - 3 + (0, 2, 1, 3)[j]))
                        elif j >= 4:
                            pe.wait_ge((gated, g_done)[j % 2], b * 4 + (i - 1))
                        hi, lo = k16(whi[slot]), k16(wlo[slot])
                        for k in range(KD):
                            last = three(dst, (hi[:, k, :], lo[:, k, :]), (act_hi[:, k, :], act_lo[:, k, :]),
                                         k == 0, k == KD - 1)
                    else:
                        d = j - 8
                        hi, lo = k4(whi[slot]), k4(wlo[slot])
                        order = [(k, t) for t in range(TB) for k in range(4)]
                        if d == 0:
                            order = [(k, t) for k in range(4) for t in range(TB)]
                        for k, t in order:
                            if d == 0 and t == 0:
                                pe.wait_ge(g_lo, b * 4 + (k + 1))
                            if d >= 2 and k == 0:
                                pe.wait_ge(o_taken, b * 16 + (O_BASE + 4 * (d - 2) + t + 1))
                            last = three(bank[(4, 0)[d % 2] + t], [gt[m][:, k, P * t:P * t + P] for m in range(2)],
                                         (hi[:, k, :], lo[:, k, :]), k == 0, k == 3)
                            if k == 3 and t < TB - 1:
                                last.then_inc(d_bank, 1)
                    last.then_inc(used, 1)
                    if first and j == 1:
                        norm_row(rcol, 2)

            feed(0)
            with pe.Fori(1, BLOCKS - 1) as b:
                feed(b)
            feed(BLOCKS - 1)


_INS = ["x", "positions", "g_mix_pre", "w_in", "g_cq", "g_ckv", "w_uq", "w_ukv", "sinks", "rel_bias", "w_o",
        "g_mix_post", "g_ffn_pre", "w_gate", "w_up", "w_down", "g_ffn_post"]


def kernel(**inputs):
    import concourse.bacc as bacc
    from concourse.bass_utils import run_bass_kernel_spmd

    nc = bacc.Bacc("TRN2", target_bir_lowering=False, num_devices=1)
    arrays, args = {}, []
    given = [(name, np.ascontiguousarray(inputs[name])) for name in _INS]
    given += [("buckets", bucket_rows()), ("inv_freq", inverse_frequencies())]
    for name, a in given:
        arrays[f"in_{name}"] = a
        args.append(nc.dram_tensor(f"in_{name}", a.shape, mybir.dt.from_np(a.dtype), kind="ExternalInput").ap())
    out = nc.dram_tensor("out_dram", (1, S, D), F32, kind="ExternalOutput").ap()
    build(nc, *args, out)
    r = run_bass_kernel_spmd(nc, [arrays], core_ids=[0])
    return r.results[0]["out_dram"]
```

```python
import math
from contextlib import ExitStack

import numpy as np

import concourse.bass as bass
from concourse import mybir

F32 = mybir.dt.float32
F32R = mybir.dt.float32r
I32 = mybir.dt.int32
ALU = mybir.AluOpType
ACT = mybir.ActivationFunctionType
AX = mybir.AxisListType

P = 128
D = 2048
S = 512
DFF = 5632
TB = S // P
KD = D // P
LORA = 512
KL = LORA // P
MLA_HEADS = 8
NOPE = 128
ROPE = 64
SWA_HEADS = 16
SWA_DIM = 64
WINDOW = 128
NUM_BUCKETS = 32
MAX_DISTANCE = 128
ROPE_THETA = 10000.0
EPS = 1e-6
NEG = -1e30
MLA_SCALE = 1.0 / math.sqrt(NOPE + ROPE)
SWA_SCALE = 1.0 / math.sqrt(SWA_DIM)

C_Q, C_KV, C_KR, C_SQ = 0, 512, 1024, 1088
C_SK = C_SQ + SWA_HEADS * SWA_DIM
C_SV = C_SK + 128
IN_PANELS = ([("ckv", j, C_KV + P * j) for j in range(KL)] + [("cq", j, C_Q + P * j) for j in range(KL)]
             + [("kr", 0, C_KR), ("sk", 0, C_SK), ("sv", 0, C_SV)]
             + [("sq", j, C_SQ + P * j) for j in range(8)])
N_IN = len(IN_PANELS)
PAIRS = MLA_HEADS // 2
Q_MLA = N_IN
Q_OUT = Q_MLA + 2 * PAIRS
Q_FFN = Q_OUT + 16
BLOCKS = DFF // 512
PER_BLOCK = 12
Q_END = Q_FFN + PER_BLOCK * BLOCKS
KG_ORDER = [2, 3, 0, 1]
CHUNK_BANKS = 6
AHEAD = 5
BIAS_W = 384
PT_W = 512 + 384 + 512
TWO_PI = 2.0 * math.pi
MAGIC = 12582912.0


def two_pi_pieces():
    point = 120
    rest = (31415926535897932384626433832795028841971 << point) // (5 * 10 ** 39)
    out = []
    for _ in range(4):
        shift = rest.bit_length() - 12
        out.append(float(rest >> shift) * 2.0 ** (shift - point))
        rest &= (1 << shift) - 1
    return out


def bucket_rows():
    dist = 255 - np.arange(BIAS_W)
    d = np.maximum(dist, 0)
    half = NUM_BUCKETS // 2
    large = half + (np.log(np.maximum(d, 1) / half) / np.log(MAX_DISTANCE / half)
                    * (NUM_BUCKETS - half)).astype(np.int32)
    bucket = np.where(d < half, d, np.minimum(large, NUM_BUCKETS - 1))
    valid = (dist >= 0) & (dist < WINDOW)
    rows = np.zeros((NUM_BUCKETS + 1, BIAS_W), np.float32)
    rows[bucket[valid], np.arange(BIAS_W)[valid]] = 1.0
    rows[NUM_BUCKETS, ~valid] = NEG
    return rows


def inverse_frequencies():
    half = ROPE // 2
    f = np.float32(ROPE_THETA) ** (-np.arange(half, dtype=np.float32) / np.float32(half))
    return np.tile(f.astype(np.float32), P // half)[:, None]


def build(nc, x, positions, g_mix_pre, w_in, g_cq, g_ckv, w_uq, w_ukv, sinks, rel_bias, w_o,
          g_mix_post, g_ffn_pre, w_gate, w_up, w_down, g_ffn_post, buckets, inv_freq, out):
    ctx = ExitStack()
    with ctx:
        base = nc.sbuf_base + 31 & ~31

        def sb(name, kb, shape, dt=F32):
            return nc.alloc_sbuf_tensor_at(name, shape, dt, offset=base + int(kb * 1024))

        def sem(name):
            return ctx.enter_context(nc.semaphore(name))

        assert nc.sbuf_top - base >= 207 * 1024
        raw = [sb(f"raw{i}", 8 * i, [P, 2048]) for i in range(2)]
        whi = [sb(f"whi{i}", 16 + 8 * i, [P, 2048], F32R) for i in range(2)]
        wlo = [sb(f"wlo{i}", 32 + 8 * i, [P, 2048], F32R) for i in range(2)]
        ident = sb("ident", 48, [P, P])
        rot = sb("rot", 48.5, [P, P])
        ones = sb("ones", 49, [P, P])
        small = sb("small", 49.5, [P, 112])
        cos_t = sb("cos_t", 50, [P, S])
        sin_t = sb("sin_t", 52, [P, S])

        at = [0]

        def cols(n):
            at[0] += n
            assert at[0] <= 112
            return small[:, at[0] - n:at[0]]

        N_GAIN = 2 * KD + 2 * KL
        gains = cols(N_GAIN)
        gpre, gffn = gains[:, 0:KD], gains[:, KD:2 * KD]
        gckv, gcq = gains[:, 2 * KD:2 * KD + KL], gains[:, 2 * KD + KL:]
        invf = cols(1)
        sink, sink_neg = cols(SWA_HEADS), cols(SWA_HEADS)
        ssum, mean, root, y0, yy, cc_, rstd = (cols(TB) for _ in range(7))
        st = sb("st", 206, [P, 4, 6, 4])
        ss4 = sb("ss4", 206.5, [P, TB, 4])

        act_hi0 = sb("act_hi0", 54, [P, KD, S], F32R)
        act_lo0 = sb("act_lo0", 86, [P, KD, S], F32R)
        xin = sb("xin", 118, [P, TB, D])
        junk0 = sb("junk0", 150, [P, D])
        relaug = sb("relaug", 162, [NUM_BUCKETS + 1, 16])
        bsel = sb("bsel", 163, [NUM_BUCKETS + 1, BIAS_W])
        brow = sb("brow", 165, [16, BIAS_W])
        gpre_rows = sb("gpre_rows", 167, [KD, P])
        gain_rows = sb("gain_rows", 167.5, [N_GAIN - KD, P])
        pos_i = sb("pos_i", 162, [P, S], I32)
        ang, kk, kh = (sb(n, 164 + 2 * i, [P, S]) for i, n in enumerate(("ang", "kk", "kh")))
        w_ms, w_y, w_a = (sb(n, 170 + 2 * i, [P, S]) for i, n in enumerate(("w_ms", "w_y", "w_a")))
        rcol0 = sb("rcol0", 176, [P, TB, P])
        rrow0 = sb("rrow0", 160, [P, S])
        ckv = [sb("ckv_hi", 118, [P, KL, S], F32R), sb("ckv_lo", 126, [P, KL, S], F32R)]
        cq = [sb("cq_hi", 134, [P, KL, S], F32R), sb("cq_lo", 142, [P, KL, S], F32R)]
        craw = [sb("craw_kv", 150, [P, KL, S]), sb("craw_q", 162, [P, KL, S])]
        skd = sb("skd", 150, [P, 2, S])
        svt = sb("svt", 154, [P, S])
        kraw = sb("kraw", 158, [P, S])
        sqt = sb("sqt", 176, [P, S])
        sq_sum = sb("sq_sum", 204, [P, S])
        sq = sb("sq", 162, [P, 8, S])
        kpad = [sb("kpad_hi", 178, [P, 2, 2, S], F32R), sb("kpad_lo", 186, [P, 2, 2, S], F32R)]
        vpad = [sb("vpad_hi", 194, [P, TB, 2, 192], F32R), sb("vpad_lo", 200, [P, TB, 2, 192], F32R)]
        mix_s = sb("mix_s", 102, [P, 8, S])
        spt = [[sb(f"spt{b}_hi", 70 + 8 * b, [P, 2, 512], F32R), sb(f"spt{b}_lo", 74 + 8 * b, [P, 2, 512], F32R)]
               for b in range(2)]
        qs = [[sb(f"qs{b}_hi", kb, [P, 2, S], F32R), sb(f"qs{b}_lo", kb + 4, [P, 2, S], F32R)]
              for b, kb in enumerate((150, 94))]
        bias_t = [sb(f"bias{b}", 54 + 8 * b, [P, 4, 256]) for b in range(2)]
        sp = [sb(f"sp{b}", kb, [P, 4, 256]) for b, kb in enumerate((58, 86, 90, 66))]
        qn = [sb("qn_hi", 70, [P, 2, S], F32R), sb("qn_lo", 74, [P, 2, S], F32R)]
        kn = [sb("kn_hi", 78, [P, 2, S], F32R), sb("kn_lo", 82, [P, 2, S], F32R)]
        vn = [sb("vn_hi", 86, [P, TB, 256], F32R), sb("vn_lo", 90, [P, TB, 256], F32R)]
        qr = [sb(f"qr{hh}", 94 + 2 * hh, [P, S], F32R) for hh in range(2)]
        mix_m = sb("mix_m", 54, [P, 8, S])
        tri = sb("tri", 98, [P, S])
        t_sb = sb("t_sb", 197, [P, S])
        t_a = sb("t_a", 199, [P, S])
        t_b = sb("t_b", 201, [P, S])
        mpt = [[sb("mpt0_hi", 150, [P, PT_W], F32R), sb("mpt0_lo", 155.5, [P, PT_W], F32R)],
               [sb("mpt1_hi", 186, [P, PT_W], F32R), sb("mpt1_lo", 191.5, [P, PT_W], F32R)]]
        kr = [sb("kr_hi", 162, [P, S], F32R), sb("kr_lo", 164, [P, S], F32R)]
        mp = [sb(f"mp{b}", 170 + 8 * b, [P, TB, S]) for b in range(2)]
        mixt = [[sb(f"mixt{kg}_hi", kb, [P, 4, S], F32R), sb(f"mixt{kg}_lo", kb + 8, [P, 4, S], F32R)]
                for kg, kb in enumerate((150, 166, 134, 118))]
        mixn = sb("mixn", 54, [P, TB, D])
        x1 = sb("x1", 86, [P, TB, D])
        gpost = sb("gpost", 182, [P, D])
        junk4 = sb("junk4", 190, [P, D])
        act_hi = sb("act_hi", 118, [P, KD, S], F32R)
        act_lo = sb("act_lo", 150, [P, KD, S], F32R)
        acc = sb("acc", 54, [P, TB, D])
        gt = [sb("gt_hi", 182, [P, 4, S], F32R), sb("gt_lo", 190, [P, 4, S], F32R)]
        sil = sb("sil", 198, [P, S])
        gf = sb("gf", 200, [P, S])
        junk6 = sb("junk6", 202, [P, S])
        rcol = sb("rcol", 202, [P, TB, P])
        rrow = sb("rrow", 204, [P, S])

        pt_ = [ctx.enter_context(nc.psum_tensor(f"bank{i}", [P, 512], F32)) for i in range(8)]
        bank = [t[:, :] for t in pt_]

        bias_row = nc.dram_tensor("bias_row", (16, BIAS_W), F32, kind="Internal").ap()
        bias_all = nc.dram_tensor("bias_all", (P, 16 * BIAS_W), F32, kind="Internal").ap()

        x_in = [sem(f"x_in{c}") for c in range(4)]
        raw_in = [sem(f"raw_in{i}") for i in range(2)]
        x_again = sem("x_again")
        y_out = sem("y_out")
        bias_src_in = sem("bias_src_in")
        cols_in = sem("cols_in")
        gpre_in = sem("gpre_in")
        rows_in = sem("rows_in")
        row_out = sem("row_out")
        rows_out = sem("rows_out")
        pos_in = sem("pos_in")
        band_in = [sem(f"band_in{b}") for b in range(2)]
        gpost_in = sem("gpost_in")
        made = sem("made")
        made_m = sem("made_m")
        acc_zero = sem("acc_zero")
        sq_added = sem("sq_added")
        x1_pool = sem("x1_pool")
        s_norm = sem("s_norm")
        y_pool = sem("y_pool")
        hi_ready = sem("hi_ready")
        sumsq_x = sem("sumsq_x")
        root_done = sem("root_done")
        squares = sem("squares")
        sines = sem("sines")
        act_h = sem("act_h")
        q_hi = sem("q_hi")
        s_exp = sem("s_exp")
        s_hi = sem("s_hi")
        s_out = sem("s_out")
        m_exp = sem("m_exp")
        m_hi = sem("m_hi")
        m_out = sem("m_out")
        o_sq = sem("o_sq")
        scaled = sem("scaled")
        silu_done = sem("silu_done")
        g_hi = sem("g_hi")
        lo_ready = sem("lo_ready")
        link_s = sem("link_s")
        brow_ready = sem("brow_ready")
        gain_cols = sem("gain_cols")
        mean_done = sem("mean_done")
        rcol_ready = sem("rcol_ready")
        rrow_ready = sem("rrow_ready")
        act_l = sem("act_l")
        angle_done = sem("angle_done")
        taken = sem("taken")
        normed = sem("normed")
        q_lo = sem("q_lo")
        s_max = sem("s_max")
        s_sink = sem("s_sink")
        s_reci = sem("s_reci")
        s_lo = sem("s_lo")
        r_in = sem("r_in")
        r_done = sem("r_done")
        m_max = sem("m_max")
        m_neg = sem("m_neg")
        m_norm = sem("m_norm")
        m_lo = sem("m_lo")
        o_taken = sem("o_taken")
        rstd_ready = sem("rstd_ready")
        x1_ready = sem("x1_ready")
        sil_normed = sem("sil_normed")
        gated = sem("gated")
        gained = sem("gained")
        g_done = sem("g_done")
        g_lo = sem("g_lo")
        y_ready = sem("y_ready")
        bias_mm = sem("bias_mm")
        gains_mm = sem("gains_mm")
        tr = sem("tr")
        rrow_mm = sem("rrow_mm")
        used = sem("used")
        sumsq_c = sem("sumsq_c")
        h_head = sem("h_head")
        sv_t = sem("sv_t")
        s_qk = sem("s_qk")
        s_t = sem("s_t")
        s_pv = sem("s_pv")
        m_proj = sem("m_proj")
        r_perm = sem("r_perm")
        m_qk = sem("m_qk")
        m_t = sem("m_t")
        m_pv = sem("m_pv")
        o_bank = sem("o_bank")
        d_bank = sem("d_bank")
        d_last = sem("d_last")

        x_v = x[0].rearrange("(t p) n -> t p n", p=P)
        x_cols = x[0].rearrange("(t p) n -> p t n", p=P)
        out_v = out[0].rearrange("(t p) n -> t p n", p=P)
        win_v = w_in[0].rearrange("(k p) n -> p k n", p=P)
        wuq_v = w_uq[0].rearrange("(k p) n -> p k n", p=P)
        wukv_v = w_ukv[0].rearrange("(k p) n -> p k n", p=P)
        wo_v = w_o[0].rearrange("(k p) n -> p k n", p=P)
        wg_v = w_gate[0].rearrange("(k p) n -> p k n", p=P)
        wu_v = w_up[0].rearrange("(k p) n -> p k n", p=P)
        wd_v = w_down[0].rearrange("(m p) n -> p m n", p=P)

        def k16(t):
            return t[:, :].rearrange("p (k n) -> p k n", k=KD)

        def k4(t, n=512):
            return t[:, 0:4 * n].rearrange("p (k n) -> p k n", k=4)

        def split_parts(q, slot):
            if not (isinstance(q, int) and Q_MLA <= q < Q_OUT and (q - Q_MLA) % 2 == 0):
                return [(whi[slot][:, :], raw[slot][:, :], wlo[slot][:, :])]
            src = k4(raw[slot], 384).rearrange("p k (h n) -> p k h n", h=2)
            out_ = []
            for c0, w, a in ((0, NOPE, 0), (NOPE, ROPE, 2 * NOPE)):
                hi, lo = (k4(t, 384)[:, :, a:a + 2 * w].rearrange("p k (h n) -> p k h n", h=2)
                          for t in (whi[slot], wlo[slot]))
                out_.append((hi, src[:, :, :, c0:c0 + w], lo))
            return out_

        def f(ap):
            return ap.bitcast(F32)

        N_H0 = KD
        N_CKV = N_H0 + KL
        N_CQ = N_CKV + KL
        N_SK = N_CQ + 4
        N_SV = N_SK + 1
        N_KR = N_SV + 1
        PER_PAIR = 8
        PROJ = 5
        PT_PARTS = ((0, 512), (512, 384), (896, 512))
        N_PAIRS = N_KR + PER_PAIR * PAIRS
        N_MIX = N_PAIRS + KD
        N_KG2 = N_PAIRS - 1 + 4
        O_BASE = 16
        UNITS = 16

        def split_hi(q, slot):
            nc.scalar.wait_ge(raw_in[slot], (q - slot) * 8 + 16)
            if not isinstance(q, int) or q >= 2:
                nc.scalar.wait_ge(used, q - 1)
            for dst, src, _ in split_parts(q, slot):
                last = nc.scalar.activation(dst, src, ACT.Copy)
            last.then_inc(hi_ready, 1)

        def split_lo(q, slot):
            nc.vector.wait_ge(hi_ready, q + 1)
            for hi, src, dst in split_parts(q, slot):
                last = nc.vector.tensor_tensor(dst, src, f(hi), ALU.subtract)
            last.then_inc(lo_ready, 1)

        def stat(u, kind):
            return st[:, u % 4, kind, :]

        MAXI, NEGM, SINKN, SINKE, TOTAL, RECI = range(6)

        def unit(u):
            return u // 4, u // 8, u % 4, (P if u % 4 == 0 else 0)

        def halves(u):
            first = 2 * u - (u + 3) // 4
            return [(kb, first + m) for m, kb in enumerate((1,) if u % 4 == 0 else (0, 1))]

        N_HALVES = halves(UNITS - 1)[-1][1] + 1

        def half_bank(h):
            return bank[4 + h % 3]

        def value_bank(h):
            return bank[3 if h % 2 and h < MLA_HEADS - 1 else 7]

        def mix_chunk(c):
            return mix_m[:, c, :] if c < 8 else mix_s[:, c - 8, :]

        def in_bank(q):
            return bank[(0, 1, 5)[q % 3] if q < N_IN - 1 else 4]

        def chunk_bank(c):
            return bank[1 + c % CHUNK_BANKS]

        def residual(src, t, a):
            return nc.vector.scalar_tensor_tensor(out=x1[:, t, a], in0=src[:, t, a], scalar=rstd[:, t:t + 1],
                                                  in1=x1[:, t, a], op0=ALU.mult, op1=ALU.add)

        def residual_times(src, t, a):
            return nc.scalar.activation(src[:, t, a], src[:, t, a], ACT.Copy, scale=rstd[:, t:t + 1])

        def residual_plus(src, t, a):
            return nc.gpsimd.tensor_tensor(x1[:, t, a], x1[:, t, a], src[:, t, a], ALU.add)

        NORM_GROUPS = ((0, 2), (2, 3), (3, 4))

        FINISH = [(t, cb) for cb in range(4) for t in (0, 1)]
        FINISH += [(t, cb) for t in (2, 3) for cb in range(4)]
        LATE = 4

        def last_down(cb):
            if cb < 2:
                slot = (Q_END - 4 + cb) % 2
                return k4(whi[slot]), k4(wlo[slot])
            c = slice(4 * cb - 8, 4 * cb - 4)
            return act_hi[:, c, :], act_lo[:, c, :]

        def shared(t):
            return slice(0, 1024 if t < TB - 1 else 512)

        def three(out_ap, a, b, first, last):
            nc.tensor.matmul(out_ap, a[0], b[0], start=first, stop=False)
            nc.tensor.matmul(out_ap, a[0], b[1], start=False, stop=False)
            return nc.tensor.matmul(out_ap, a[1], b[0], start=False, stop=last)

        block = ctx.enter_context(nc.Block())

        @block.sync
        def _(sp_):
            def fetch(q, src, view):
                if q >= 2:
                    sp_.wait_ge(lo_ready, q - 1)
                sp_.dma_start(view, src).then_inc(raw_in[q % 2], 16)

            for q, (_, _, c) in enumerate(IN_PANELS):
                fetch(q, win_v[:, :, c:c + P], k16(raw[q % 2]))
                if q == 0:
                    for n in range(4):
                        cols_n = slice(512 * n, 512 * n + 512)
                        sp_.dma_start(xin[:, :, cols_n], x_cols[:, :, cols_n]).then_inc(x_in[n], 16)
            for p in range(PAIRS):
                q = Q_MLA + 2 * p
                fetch(q, wuq_v[:, :, 384 * p:384 * p + 384], k4(raw[q % 2], 384))
                fetch(q + 1, wukv_v[:, :, 512 * p:512 * p + 512], k4(raw[(q + 1) % 2]))
            for i in range(16):
                q = Q_OUT + i
                cb, kg = i // 4, KG_ORDER[i % 4]
                fetch(q, wo_v[:, 4 * kg:4 * kg + 4, 512 * cb:512 * cb + 512], k4(raw[q % 2]))
                if i == 3:
                    sp_.wait_ge(act_l, N_MIX)
                    for t in range(TB):
                        sp_.dma_start(x1[:, t, :], x_v[t]).then_inc(x_again, 16)

            def fetch_block(b):
                for j in range(PER_BLOCK):
                    slot = (Q_FFN + j) % 2
                    sp_.wait_ge(lo_ready, b * PER_BLOCK + (Q_FFN + j - 1))
                    if j < 8:
                        src = (wg_v, wu_v)[j % 2][:, :, bass.ds(b * 512 + P * (j // 2), P)]
                        sp_.dma_start(k16(raw[slot]), src).then_inc(raw_in[slot], 16)
                    else:
                        src = wd_v[:, bass.ds(b * 4, 4), 512 * (j - 8):512 * (j - 8) + 512]
                        sp_.dma_start(k4(raw[slot]), src).then_inc(raw_in[slot], 16)

            with sp_.Fori(0, BLOCKS - 1) as b:
                fetch_block(b)
            fetch_block(BLOCKS - 1)
            sp_.wait_ge(lo_ready, Q_END - 1)
            sp_.dma_start(raw[Q_END % 2][:, :], g_ffn_post.broadcast_to([P, D])).then_inc(raw_in[Q_END % 2], 16)
            for t in range(TB):
                sp_.wait_ge(y_ready, t + 1)
                w = shared(t).stop
                sp_.dma_start(out_v[t][:, w:D], x1[:, t, w:D]).then_inc(y_out, 16)
                sp_.wait_ge(y_pool, t + 1)
                sp_.dma_start(out_v[t][:, 0:w], x1[:, t, 0:w]).then_inc(y_out, 16)
            sp_.wait_ge(y_out, 16 * 2 * TB)

        @block.gpsimd
        def _(pool):
            n = [0]

            def make(ins):
                n[0] += 1
                ins.then_inc(made, 1)

            make(nc.gpsimd.memset(ident[:, :], 0.0))
            make(nc.gpsimd.memset(rot[:, :], 0.0))
            make(nc.gpsimd.memset(ones[:, :], 1.0))
            pool.wait_ge(made, 3)
            make(nc.gpsimd.memset(relaug[NUM_BUCKETS:NUM_BUCKETS + 1, :], 1.0))
            pool.wait_ge(made, 4)
            make(nc.gpsimd.affine_select(out=ident[:, :], in_=ident[:, :], compare_op=ALU.not_equal, fill=1.0,
                                         base=0, pattern=[[-1, P]], channel_multiplier=1))
            rv = rot[:, :].rearrange("p (b h r) -> p b h r", b=2, h=2)
            make(nc.gpsimd.affine_select(out=rv[:, :, 0, :], in_=rv[:, :, 0, :], compare_op=ALU.not_equal,
                                         fill=-1.0, base=-32, pattern=[[-64, 2], [-1, 32]], channel_multiplier=1))
            pool.wait_ge(made, 6)
            make(nc.gpsimd.affine_select(out=rv[:, :, 1, :], in_=rv[:, :, 1, :], compare_op=ALU.not_equal,
                                         fill=1.0, base=0, pattern=[[-64, 2], [-1, 32]], channel_multiplier=1))
            for t in (*kpad, vpad[0]):
                make(nc.gpsimd.memset(f(t[:]), 0.0))
            for latent in range(2):
                for j in range(1, KL):
                    pool.wait_ge(squares, KL * latent + j + 1)
                    if j > 1:
                        pool.wait_ge(sq_added, (KL - 1) * latent + j - 1)
                    nc.gpsimd.tensor_tensor(sq_sum[:, :], sq_sum[:, :], sqt[:, :], ALU.add).then_inc(sq_added, 1)
            pool.wait_ge(sumsq_c, 2)
            make(nc.gpsimd.memset(f(vpad[1][:]), 0.0))
            for u in range(UNITS):
                lo = unit(u)[3]
                pool.wait_ge(s_reci, u + 1)
                blk = sp[u % 4][:, :, lo:256]
                nc.gpsimd.tensor_tensor(blk, blk, stat(u, RECI).unsqueeze(2).broadcast_to([P, 4, 256 - lo]),
                                        ALU.mult).then_inc(s_norm, 1)
            pool.wait_ge(s_out, UNITS)
            pool.wait_ge(used, N_IN)
            nc.gpsimd.memset(tri[:, :], 0.0).then_inc(made_m, 1)
            pool.wait_ge(made_m, 1)
            nc.gpsimd.affine_select(out=tri[:, 384:512], in_=tri[:, 384:512], compare_op=ALU.is_ge, fill=NEG,
                                    base=0, pattern=[[-1, P]], channel_multiplier=1).then_inc(made_m, 1)
            for t in mp:
                nc.gpsimd.memset(t[:, 2, 384:512], 0.0).then_inc(made_m, 1)
            pool.wait_ge(hi_ready, Q_FFN + 1)
            pool.wait_ge(lo_ready, Q_FFN)
            hi, src, low = split_parts(Q_FFN, Q_FFN % 2)[0]
            nc.gpsimd.tensor_tensor(low, src, f(hi), ALU.subtract).then_inc(lo_ready, 1)
            pool.wait_ge(x_again, 16 * TB)
            for t in range(TB):
                for n in (2, 3):
                    pool.wait_ge(scaled, 2 * t + n - 1)
                    residual_plus(mixn, t, slice(512 * n, 512 * n + 512)).then_inc(x1_pool, 1)
            pool.wait_ge(x1_ready, 2 * TB)
            pool.wait_ge(x1_pool, 2 * TB)
            nc.gpsimd.memset(acc[:], 0.0).then_inc(acc_zero, 1)
            for t in range(TB):
                pool.wait_ge(scaled, 2 * TB + t + 1)
                residual_plus(acc, t, shared(t)).then_inc(y_pool, 1)

        @block.scalar
        def _(act):
            def copy_hi(dst, src, scale=None):
                if scale is None:
                    nc.scalar.activation(dst, src, ACT.Copy).then_inc(act_h, 1)
                else:
                    nc.scalar.activation(dst, src, ACT.Copy, scale=scale).then_inc(act_h, 1)

            def token_squares(src, junk):
                for t in range(TB):
                    if sumsqs[0]:
                        act.wait_ge(sumsq_x, sumsqs[0])
                    nc.scalar.activation(junk[:, :], src[:, t, :], ACT.Square,
                                         accum_out=ssum[:, t:t + 1]).then_inc(sumsq_x, 1)
                    sumsqs[0] += 1

            sumsqs = [0]

            def norm_root(t, norms_before):
                for n, (t0, t1) in enumerate(NORM_GROUPS):
                    if t1 == t + 1:
                        act.wait_ge(mean_done, norms_before + n + 1)
                        nc.scalar.activation(root[:, t0:t1], mean[:, t0:t1], ACT.Sqrt).then_inc(root_done, 1)

            act.dma_start(gpre_rows[:, :], g_mix_pre[0].rearrange("(c p) -> c p", p=P)).then_inc(gpre_in, 16)
            at_row = 0
            for src in (g_ffn_pre, g_ckv, g_cq):
                rows = src[0].rearrange("(c p) -> c p", p=P)
                act.dma_start(gain_rows[at_row:at_row + rows.shape[0], :], rows).then_inc(rows_in, 16)
                at_row += rows.shape[0]
            act.dma_start(relaug[0:NUM_BUCKETS, :], rel_bias).then_inc(bias_src_in, 16)
            act.dma_start(bsel[:, :], buckets).then_inc(bias_src_in, 16)
            act.dma_start(invf, inv_freq).then_inc(cols_in, 16)
            act.dma_start(sink, sinks.broadcast_to([P, SWA_HEADS])).then_inc(cols_in, 16)

            act.wait_ge(made, 3)
            nc.scalar.activation(ss4[:, 0, 0:1], ones[:, 0:1], ACT.Copy)
            split_hi(0, 0)
            act.wait_ge(gain_cols, 1)
            for c in range(KD):
                if c == 12:
                    split_hi(1, 1)
                act.wait_ge(tr, c + 1)
                copy_hi(act_hi0[:, c, :], chunk_bank(c), gpre[:, c:c + 1])
            for n in range(4):
                act.wait_ge(x_in[n], 16)
            token_squares(xin, junk0)
            act.wait_ge(mean_done, 1)
            nc.scalar.activation(root[:, :], mean[:, :], ACT.Sqrt).then_inc(root_done, 1)
            split_hi(2, 0)
            act.wait_ge(brow_ready, 1)
            act.dma_start(bias_row, brow[:, :]).then_inc(row_out, 16)
            act.wait_ge(row_out, 16)
            act.dma_start(bias_all, bias_row.rearrange("h w -> (h w)").unsqueeze(0)
                          .broadcast_to([P, 16 * BIAS_W])).then_inc(rows_out, 16)
            act.dma_start(pos_i[:, :], positions.broadcast_to([P, S])).then_inc(pos_in, 16)

            def split_queries_hi(gh, half):
                nc.scalar.activation(qs[gh % 2][0][:, half, :], sq[:, 2 * gh + half, :],
                                     ACT.Copy).then_inc(q_hi, 1)

            def load_band(gh):
                act.dma_start(bias_t[gh % 2][:, :, :],
                              bass.AP(tensor=bias_all.tensor, offset=4 * gh * BIAS_W + 127,
                                      ap=[[16 * BIAS_W - 1, P], [BIAS_W, 4], [1, 256]])
                              ).then_inc(band_in[gh % 2], 16)

            def window(s):
                if s >= 5:
                    u = s - 5
                    gh, _, n, _ = unit(u)
                    act.wait_ge(s_pv, u + 1)
                    nc.scalar.activation(mix_s[:, 2 * gh:2 * gh + 2, P * n:P * n + P],
                                         bank[7][:, 0:256].rearrange("p (c n) -> p c n", c=2),
                                         ACT.Copy).then_inc(s_out, 1)
                if 3 <= s < UNITS + 3:
                    u = s - 3
                    if u >= 2:
                        act.wait_ge(s_pv, u - 1)
                    for kb, h in halves(u):
                        act.wait_ge(s_t, h + 1)
                        nc.scalar.activation(spt[u % 2][0][:, kb, :], half_bank(h), ACT.Copy).then_inc(s_hi, 1)
                if s < UNITS:
                    gh, _, n, lo = unit(s)
                    act.wait_ge(s_max, s + 1)
                    for hd in range(4):
                        nc.scalar.activation(sp[s % 4][:, hd, lo:256], sp[s % 4][:, hd, lo:256], ACT.Exp,
                                             bias=stat(s, NEGM)[:, hd:hd + 1], scale=SWA_SCALE,
                                             accum_out=stat(s, TOTAL)[:, hd:hd + 1])
                    act.wait_ge(s_sink, s + 1)
                    nc.scalar.activation(stat(s, SINKE), stat(s, SINKN), ACT.Exp).then_inc(s_exp, 1)
                    if n in (1, 2) and 1 <= gh < 3:
                        act.wait_ge(s_qk, 4 * gh)
                        split_queries_hi(gh + 1, n - 1)
                    if n == 3 and gh + 2 < 4:
                        load_band(gh + 2)

            for q in range(N_IN):
                what, j, _ = IN_PANELS[q]
                if q == N_IN - 1:
                    act.wait_ge(rows_out, 16)
                    act.wait_ge(h_head, 1)
                    load_band(0)
                    window(0)
                    window(1)
                elif q:
                    split_hi(q + 2, q % 2)
                if what in ("ckv", "cq"):
                    act.wait_ge(taken, q + 1)
                    n = q // KL
                    if j == 0 and n:
                        act.wait_ge(sumsq_c, n)
                    if j > 1:
                        act.wait_ge(sq_added, (KL - 1) * n + j - 1)
                    nc.scalar.activation((sqt if j else sq_sum)[:, :], craw[n][:, j, :],
                                         ACT.Square).then_inc(squares, 1)
                if q == 2:
                    act.wait_ge(angle_done, 1)
                    nc.scalar.activation(sin_t[:, :], ang[:, :], ACT.Sin).then_inc(sines, 1)
                    nc.scalar.activation(kk[:, :], ang[:, :], ACT.Sin, scale=0.5).then_inc(sines, 1)
                if q in (KL, 2 * KL):
                    n = q // KL - 1
                    act.wait_ge(mean_done, n + 2)
                    nc.scalar.activation(w_y[:, :], w_ms[:, :], ACT.Sqrt).then_inc(root_done, 1)
                    for i in range(KL):
                        act.wait_ge(normed, KL * n + i + 1)
                        copy_hi((ckv, cq)[n][0][:, i, :], craw[n][:, i, :])
                if what == "sk":
                    act.wait_ge(made, 11)
                    act.wait_ge(taken, q + 1)
                    for i in range(4):
                        g, e = i // 2, i % 2
                        rows = slice(64 * e, 64 * e + 64)
                        copy_hi(kpad[0][rows, g, e, :], skd[rows, g, :])
                if q == N_IN - 4:
                    act.wait_ge(taken, N_IN - 6)
                    split_queries_hi(0, 0)
                    split_queries_hi(0, 1)
                if q == N_IN - 8:
                    act.wait_ge(sv_t, 1)
                    copy_hi(vpad[0][:, :, :, 64:128], bank[4].rearrange("p (b g d) -> p b g d", b=TB, g=2))

            act.wait_ge(used, N_IN)
            load_band(1)
            split_queries_hi(1, 0)
            split_queries_hi(1, 1)
            for s in range(2, UNITS + 5):
                window(s)
                if s == UNITS + 1:
                    split_hi(N_IN + 1, (N_IN + 1) % 2)

            act.wait_ge(r_done, 1)
            copy_hi(kr[0][:, :], t_a[:, :])

            def copy_from(waited, value, dst, b):
                act.wait_ge(waited, value)
                copy_hi(dst, b)

            def exponentials(h):
                act.wait_ge(m_neg, h + 1)
                for i in range(TB):
                    blk = mp[h % 2][:, i, 0:P * (i + 1)]
                    nc.scalar.activation(blk, blk, ACT.Exp, bias=stat(h, NEGM)[:, i:i + 1],
                                         scale=MLA_SCALE, accum_out=stat(h, TOTAL)[:, i:i + 1]
                                         ).then_inc(m_exp, 1)

            def transposed_hi(h):
                if h >= 2:
                    act.wait_ge(m_pv, h - 1)
                for i, (o, w) in enumerate(PT_PARTS):
                    act.wait_ge(m_t, 3 * h + i + 1)
                    nc.scalar.activation(mpt[h % 2][0][:, o:o + w], bank[4 + i][:, 0:w],
                                         ACT.Copy).then_inc(m_hi, 1)

            def head_out(h):
                act.wait_ge(m_pv, h + 1)
                nc.scalar.activation(mix_m[:, h, :], value_bank(h), ACT.Copy).then_inc(m_out, 1)

            def queries_hi(p, hh):
                if p:
                    act.wait_ge(m_qk, 4 * 2 * p)
                if hh == 0:
                    copy_from(m_proj, PROJ * p + 2, qn[0][:, 0, :], bank[1])
                else:
                    copy_from(used, Q_MLA + 2 * p + 1, qn[0][:, 1, :], bank[2])

            def mix_hi(kg):
                for k in range(4):
                    copy_hi(mixt[kg][0][:, k, :], mix_chunk(4 * kg + k))

            queries_hi(0, 0)
            queries_hi(0, 1)
            for p in range(PAIRS):
                q, proj = Q_MLA + 2 * p, PROJ * p
                split_hi(q + 2, q % 2)
                copy_from(m_proj, proj + 3, kn[0][:, 0, :], bank[0])
                copy_from(m_proj, proj + 4, kn[0][:, 1, :], bank[1])
                if p:
                    act.wait_ge(m_pv, 2 * p)
                copy_from(m_proj, proj + 5, vn[0][:, 0:2, :], bank[2].rearrange("p (t n) -> p t n", t=2))
                for hh in range(2):
                    copy_from(r_done, p + 2, qr[hh][64 * hh:64 * hh + 64, :], t_a[64 * hh:64 * hh + 64, :])
                if p == PAIRS - 1:
                    act.wait_ge(s_out, UNITS)
                    mix_hi(2)
                exponentials(2 * p)
                copy_from(used, q + 2, vn[0][:, 2:4, :], bank[7].rearrange("p (t n) -> p t n", t=2))
                transposed_hi(2 * p)
                exponentials(2 * p + 1)
                split_hi(q + 3, (q + 1) % 2)
                head_out(2 * p)
                transposed_hi(2 * p + 1)
                if p < PAIRS - 1:
                    queries_hi(p + 1, 0)
                else:
                    mix_hi(3)
                head_out(2 * p + 1)
                if p < PAIRS - 1:
                    queries_hi(p + 1, 1)

            act.dma_start(gpost[:, :], g_mix_post.broadcast_to([P, D])).then_inc(gpost_in, 16)
            act.wait_ge(m_out, MLA_HEADS)
            mix_hi(0)
            mix_hi(1)
            for i in range(16):
                q = Q_OUT + i
                if i % 4 == 3:
                    for t in range(TB):
                        if t < TB - 1:
                            act.wait_ge(o_bank, 3 * (i // 4) + t + 1)
                        else:
                            act.wait_ge(used, q + 1)
                        if i > 3 or t:
                            act.wait_ge(o_sq, 4 * (i // 4) + t)
                        nc.scalar.activation(junk4[:, 0:512], bank[4 * (i // 4 % 2) + t], ACT.Square,
                                             accum_out=ss4[:, t, i // 4:i // 4 + 1]).then_inc(o_sq, 1)
                        if i == 15:
                            norm_root(t, 3)
                            for u in ((), (0,), (1,), (2, 3))[t]:
                                act.wait_ge(o_taken, O_BASE - TB + u + 1)
                                act.wait_ge(rstd_ready, 1 + max(0, u - 1))
                                for n in (2, 3):
                                    residual_times(mixn, u, slice(512 * n, 512 * n + 512)).then_inc(scaled, 1)
                if i < 15:
                    split_hi(q + 2, q % 2)
            for c in range(KD):
                if c == 8:
                    split_hi(Q_FFN + 1, (Q_FFN + 1) % 2)
                act.wait_ge(tr, KD + c + 1)
                copy_hi(act_hi[:, c, :], chunk_bank(c), gffn[:, c:c + 1])
            act.wait_ge(x1_ready, 2 * TB)
            act.wait_ge(x1_pool, 2 * TB)
            act.wait_ge(o_sq, 16)
            token_squares(x1, junk4)
            act.wait_ge(mean_done, 7)
            nc.scalar.activation(root[:, :], mean[:, :], ACT.Sqrt).then_inc(root_done, 1)
            split_hi(Q_FFN + 2, Q_FFN % 2)

            def feed(b, panels=PER_BLOCK):
                for j in range(panels):
                    q = b * PER_BLOCK + (Q_FFN + j)
                    slot = (Q_FFN + j) % 2
                    i = j // 2
                    if j < 8 and j % 2 == 0:
                        act.wait_ge(gated, b * 4 + (i + 1))
                        nc.scalar.activation(sil[:, :], sil[:, :], ACT.Silu).then_inc(silu_done, 1)
                    elif j < 8:
                        act.wait_ge(g_done, b * 4 + (i + 1))
                        nc.scalar.activation(gt[0][:, i, :], gf[:, :], ACT.Copy).then_inc(g_hi, 1)
                    if not isinstance(b, int) or q > Q_FFN:
                        split_hi(q + 2, slot)

            feed(0)
            with act.Fori(1, BLOCKS - 1) as b:
                feed(b)
            feed(BLOCKS - 1, 8)

            def last_hi(cb):
                q = Q_END - 4 + cb
                act.wait_ge(raw_in[q % 2], (q - q % 2) * 8 + 16)
                act.wait_ge(used, Q_END - 4)
                nc.scalar.activation(last_down(cb)[0], k4(raw[q % 2]), ACT.Copy).then_inc(hi_ready, 1)

            last_hi(2)
            for i, (t, cb) in enumerate(FINISH):
                if i == LATE - 1:
                    last_hi(3)
                act.wait_ge(o_taken, O_BASE + 16 * (BLOCKS - 1) + i + 1)
                act.wait_ge(o_sq, 16 + i)
                nc.scalar.activation(junk6[:, :], acc[:, t, 512 * cb:512 * cb + 512], ACT.Square,
                                     accum_out=ss4[:, t, cb:cb + 1]).then_inc(o_sq, 1)
                if cb == 3:
                    act.wait_ge(mean_done, 7 + t + 1)
                    nc.scalar.activation(root[:, t:t + 1], mean[:, t:t + 1], ACT.Sqrt).then_inc(root_done, 1)
                    act.wait_ge(gained, 4 * t + 4)
                    act.wait_ge(rstd_ready, 3 + t + 1)
                    residual_times(acc, t, shared(t)).then_inc(scaled, 1)

        @block.vector
        def _(dve):
            chain = [0]

            def link(ins):
                chain[0] += 1
                ins.then_inc(link_s, 1)
                dve.wait_ge(link_s, chain[0])

            def sub_lo(dst, src, hi):
                lows[0] += 1
                dve.wait_ge(act_h, lows[0])
                nc.vector.tensor_tensor(dst, src, f(hi), ALU.subtract).then_inc(act_l, 1)

            def scaled_lo(dst, src, g, hi):
                lows[0] += 1
                dve.wait_ge(act_h, lows[0])
                nc.vector.scalar_tensor_tensor(out=dst, in0=src, scalar=g, in1=f(hi), op0=ALU.mult,
                                               op1=ALU.subtract).then_inc(act_l, 1)

            lows = [0]

            def inverse_root(v, r, y, a, c, res):
                link(nc.vector.reciprocal(y, r))
                link(nc.vector.tensor_tensor(a, v, y, ALU.mult))
                link(nc.vector.tensor_tensor(a, a, y, ALU.mult))
                link(nc.vector.tensor_scalar(c, a, -0.5, 1.5, ALU.mult, ALU.add))
                return nc.vector.tensor_tensor(res, y, c, ALU.mult)

            dve.wait_ge(gains_mm, 1)
            nc.vector.tensor_copy(gpre, bank[7][:, 0:KD]).then_inc(gain_cols, 1)

            def norm_column(col, count):
                dve.wait_ge(sumsq_x, TB * count)
                nc.vector.tensor_scalar(mean, ssum, 1.0 / D, EPS, ALU.mult, ALU.add).then_inc(mean_done, 1)
                dve.wait_ge(root_done, (1, 7)[count - 1])
                link(inverse_root(mean, root, y0, yy, cc_, rstd))
                for t in range(TB):
                    last = nc.vector.tensor_scalar(col[:, t, :], ones[:, :], rstd[:, t:t + 1], None, ALU.mult)
                last.then_inc(rcol_ready, 1)

            def take_norm_row(row, count):
                dve.wait_ge(rrow_mm, count)
                nc.vector.tensor_copy(row[:, :], bank[7]).then_inc(rrow_ready, 1)
                dve.wait_ge(rrow_ready, count)

            split_lo(0, 0)
            for c in range(KD):
                if c == 12:
                    split_lo(1, 1)
                scaled_lo(act_lo0[:, c, :], chunk_bank(c), gpre[:, c:c + 1], act_hi0[:, c, :])
            dve.wait_ge(cols_in, 32)
            link(nc.vector.tensor_scalar(sink_neg, sink, -1.0, None, ALU.mult))

            dve.wait_ge(gains_mm, 2)
            nc.vector.tensor_copy(gains[:, KD:], bank[7][:, KD:N_GAIN]).then_inc(gain_cols, 1)
            dve.wait_ge(bias_mm, 1)
            nc.vector.tensor_scalar(brow[:, :], bank[6][0:16, 0:BIAS_W], 1.0 / SWA_SCALE, None,
                                    ALU.mult).then_inc(brow_ready, 1)

            norm_column(rcol0, 1)
            split_lo(2, 0)
            take_norm_row(rrow0, 1)

            def turns():
                dve.wait_ge(pos_in, 16)
                link(nc.vector.tensor_copy(ang[:, :], pos_i[:, :]))
                link(nc.vector.tensor_scalar(ang[:, :], ang[:, :], invf, None, ALU.mult))
                link(nc.vector.tensor_scalar(kk[:, :], ang[:, :], 1.0 / TWO_PI, MAGIC, ALU.mult, ALU.add))
                link(nc.vector.tensor_scalar(kk[:, :], kk[:, :], MAGIC, None, ALU.subtract))
                link(nc.vector.tensor_scalar(kh[:, :], kk[:, :], 1.0 / 2048, MAGIC, ALU.mult, ALU.add))
                link(nc.vector.tensor_scalar(kh[:, :], kh[:, :], MAGIC, None, ALU.subtract))
                link(nc.vector.scalar_tensor_tensor(out=kk[:, :], in0=kh[:, :], scalar=-2048.0, in1=kk[:, :],
                                                    op0=ALU.mult, op1=ALU.add))

            def angles():
                for c in two_pi_pieces():
                    link(nc.vector.scalar_tensor_tensor(out=ang[:, :], in0=kh[:, :], scalar=-2048.0 * c,
                                                        in1=ang[:, :], op0=ALU.mult, op1=ALU.add))
                    link(nc.vector.scalar_tensor_tensor(out=ang[:, :], in0=kk[:, :], scalar=-c, in1=ang[:, :],
                                                        op0=ALU.mult, op1=ALU.add))
                nc.vector.tensor_scalar(ang[:, :], ang[:, :], 3.1415925, -3.1415925, ALU.min,
                                        ALU.max).then_inc(angle_done, 1)

            def latent_norm(n):
                dve.wait_ge(sumsq_c, n + 1)
                nc.vector.tensor_scalar(w_ms[:, :], bank[2 + n], 1.0 / LORA, EPS, ALU.mult,
                                        ALU.add).then_inc(mean_done, 1)
                dve.wait_ge(root_done, n + 2)
                link(inverse_root(w_ms[:, :], w_y[:, :], w_y[:, :], w_a[:, :], w_a[:, :], w_y[:, :]))
                for i in range(KL):
                    nc.vector.scalar_tensor_tensor(out=craw[n][:, i, :], in0=craw[n][:, i, :],
                                                   scalar=(gckv, gcq)[n][:, i:i + 1], in1=w_y[:, :],
                                                   op0=ALU.mult, op1=ALU.mult).then_inc(normed, 1)
                for i in range(KL):
                    sub_lo((ckv, cq)[n][1][:, i, :], craw[n][:, i, :], (ckv, cq)[n][0][:, i, :])

            def split_queries_lo(gh, half):
                dve.wait_ge(q_hi, 2 * gh + half + 1)
                nc.vector.tensor_tensor(qs[gh % 2][1][:, half, :], sq[:, 2 * gh + half, :],
                                        f(qs[gh % 2][0][:, half, :]), ALU.subtract).then_inc(q_lo, 1)

            def window(s):
                def reciprocals():
                    if 1 <= s < UNITS + 1:
                        u = s - 1
                        dve.wait_ge(s_exp, u + 1)
                        link(nc.vector.tensor_tensor(stat(u, MAXI), stat(u, TOTAL), stat(u, SINKE), ALU.add))
                        nc.vector.reciprocal(stat(u, RECI), stat(u, MAXI)).then_inc(s_reci, 1)

                if s == UNITS:
                    reciprocals()
                if s < UNITS:
                    gh, _, n, lo = unit(s)
                    dve.wait_ge(s_qk, s + 1)
                    if n == 0:
                        dve.wait_ge(band_in[gh % 2], 16 * (gh // 2 + 1))
                    if s >= 4:
                        dve.wait_ge(s_t, halves(s - 4)[-1][1] + 1)
                    for hd in range(4):
                        if hd == 2:
                            reciprocals()
                        scores = bank[(s + 1) % 2 * 2 + hd // 2].rearrange("p (e k) -> p e k", e=2)[:, hd % 2, lo:256]
                        last = nc.vector.tensor_tensor_reduce(
                            sp[s % 4][:, hd, lo:256], scores, bias_t[gh % 2][:, hd, lo:256], 1.0, -3e38,
                            ALU.add, ALU.max, stat(s, MAXI)[:, hd:hd + 1])
                    link(last)
                    heads = slice(4 * gh, 4 * gh + 4)
                    nc.vector.scalar_tensor_tensor(out=stat(s, NEGM), in0=stat(s, MAXI), scalar=-SWA_SCALE,
                                                   in1=sink_neg[:, heads], op0=ALU.mult,
                                                   op1=ALU.min).then_inc(s_max, 1)
                    dve.wait_ge(s_max, s + 1)
                    nc.vector.tensor_tensor(stat(s, SINKN), stat(s, NEGM), sink[:, heads],
                                            ALU.add).then_inc(s_sink, 1)
                if s >= 3:
                    u = s - 3
                    for kb, h in halves(u):
                        dve.wait_ge(s_hi, h + 1)
                        nc.vector.tensor_tensor(spt[u % 2][1][:, kb, :], half_bank(h),
                                                f(spt[u % 2][0][:, kb, :]), ALU.subtract).then_inc(s_lo, 1)
                if 4 < s < 12 and s % 4 >= 2:
                    split_queries_lo(s // 4 + 1, s % 4 - 2)

            for q in range(N_IN):
                what, j, _ = IN_PANELS[q]
                b = in_bank(q)
                if q == N_IN - 1:
                    dve.wait_ge(h_head, 2)
                    window(0)
                    window(1)

                def take(dst, rows=slice(0, P)):
                    return nc.vector.tensor_tensor(dst, b[rows, :], rrow0[rows, :], ALU.mult)

                dve.wait_ge(used, q + 1)
                if what in ("ckv", "cq"):
                    take(craw[q // KL][:, j, :]).then_inc(taken, 1)
                elif what == "kr":
                    take(kraw[0:64, :], slice(0, 64))
                    take(kraw[64:128, :], slice(0, 64)).then_inc(taken, 1)
                elif what == "sk":
                    for i in range(4):
                        g, e = i // 2, i % 2
                        last = take(skd[64 * e:64 * e + 64, g, :], slice(64 * g, 64 * g + 64))
                    last.then_inc(taken, 1)
                elif what == "sv":
                    take(svt[:, :]).then_inc(taken, 1)
                else:
                    take(sq[:, j, :]).then_inc(taken, 1)
                if 0 < q < N_IN - 1:
                    split_lo(q + 2, q % 2)
                if q == 1:
                    turns()
                if q == 2:
                    angles()
                if q == 3:
                    dve.wait_ge(sines, 2)
                    link(nc.vector.tensor_tensor(kk[:, :], kk[:, :], kk[:, :], ALU.mult))
                    link(nc.vector.tensor_scalar(cos_t[:, :], kk[:, :], -2.0, 1.0, ALU.mult, ALU.add))
                if q in (KL, 2 * KL):
                    latent_norm(q // KL - 1)
                if q == N_IN - 4:
                    split_queries_lo(0, 0)
                    split_queries_lo(0, 1)
                if what == "sk":
                    for i in range(4):
                        g, e = i // 2, i % 2
                        rows = slice(64 * e, 64 * e + 64)
                        sub_lo(kpad[1][rows, g, e, :], skd[rows, g, :], kpad[0][rows, g, e, :])
                if q == N_IN - 8:
                    sub_lo(vpad[1][:, :, :, 64:128], bank[4].rearrange("p (b g d) -> p b g d", b=TB, g=2),
                           vpad[0][:, :, :, 64:128])

            for s in range(2, UNITS + 3):
                window(s)
                if s == 2:
                    split_queries_lo(1, 0)
                    split_queries_lo(1, 1)
            split_lo(N_IN + 1, (N_IN + 1) % 2)

            def rotate(src, n):
                link(nc.vector.tensor_tensor(t_a[:, :], src, cos_t[:, :], ALU.mult))
                dve.wait_ge(r_perm, n + 1)
                link(nc.vector.tensor_tensor(t_b[:, :], bank[7], sin_t[:, :], ALU.mult))
                nc.vector.tensor_tensor(t_a[:, :], t_a[:, :], t_b[:, :], ALU.add).then_inc(r_done, 1)

            dve.wait_ge(s_pv, UNITS)
            rotate(kraw[:, :], 0)
            sub_lo(kr[1][:, :], t_a[:, :], kr[0][:, :])

            def maxima(h):
                if h == 0:
                    dve.wait_ge(made_m, 4)
                if h >= 2:
                    dve.wait_ge(m_t, 3 * (h - 1))
                for i in range(TB):
                    w = P * (i + 1)
                    dve.wait_ge(m_qk, 4 * h + i + 1)
                    nc.vector.tensor_tensor_reduce(
                        mp[h % 2][:, i, 0:w], bank[i][:, 0:w], tri[:, 384 - P * i:512], 1.0, -3e38,
                        ALU.add, ALU.max, stat(h, MAXI)[:, i:i + 1]).then_inc(m_max, 1)
                dve.wait_ge(m_max, 4 * h + 4)
                nc.vector.tensor_scalar(stat(h, NEGM), stat(h, MAXI), -MLA_SCALE, None,
                                        ALU.mult).then_inc(m_neg, 1)

            def probabilities(h):
                dve.wait_ge(m_exp, 4 * h + 4)
                link(nc.vector.reciprocal(stat(h, RECI), stat(h, TOTAL)))
                for i in range(TB):
                    blk = mp[h % 2][:, i, 0:P * (i + 1)]
                    nc.vector.tensor_scalar(blk, blk, stat(h, RECI)[:, i:i + 1], None,
                                            ALU.mult).then_inc(m_norm, 1)

            def transposed_lo(h):
                for i, (o, w) in enumerate(PT_PARTS):
                    dve.wait_ge(m_hi, 3 * h + i + 1)
                    nc.vector.tensor_tensor(mpt[h % 2][1][:, o:o + w], bank[4 + i][:, 0:w],
                                            f(mpt[h % 2][0][:, o:o + w]), ALU.subtract).then_inc(m_lo, 1)

            def rotary_in(p):
                dve.wait_ge(m_proj, PROJ * p + 1)
                nc.vector.tensor_copy(t_sb[:, :], bank[0]).then_inc(r_in, 1)

            def queries_lo(hh):
                sub_lo(qn[1][:, hh, :], bank[1 + hh], qn[0][:, hh, :])

            def mix_lo(kg):
                for k in range(4):
                    sub_lo(mixt[kg][1][:, k, :], mix_chunk(4 * kg + k), mixt[kg][0][:, k, :])

            rotary_in(0)
            queries_lo(0)
            queries_lo(1)
            for p in range(PAIRS):
                q = Q_MLA + 2 * p
                split_lo(q + 2, q % 2)
                sub_lo(kn[1][:, 0, :], bank[0], kn[0][:, 0, :])
                dve.wait_ge(r_in, p + 1)
                rotate(t_sb[:, :], p + 1)
                sub_lo(kn[1][:, 1, :], bank[1], kn[0][:, 1, :])
                sub_lo(vn[1][:, 0:2, :], bank[2].rearrange("p (t n) -> p t n", t=2), vn[0][:, 0:2, :])
                for hh in range(2):
                    rows, other = slice(64 * hh, 64 * hh + 64), slice(64 - 64 * hh, 128 - 64 * hh)
                    sub_lo(qr[hh][other, :], t_a[rows, :], qr[hh][rows, :])
                maxima(2 * p)
                if p == PAIRS - 1:
                    mix_lo(2)
                probabilities(2 * p)
                sub_lo(vn[1][:, 2:4, :], bank[7].rearrange("p (t n) -> p t n", t=2), vn[0][:, 2:4, :])
                maxima(2 * p + 1)
                transposed_lo(2 * p)
                if p < PAIRS - 1:
                    rotary_in(p + 1)
                probabilities(2 * p + 1)
                split_lo(q + 3, (q + 1) % 2)
                transposed_lo(2 * p + 1)
                if p < PAIRS - 1:
                    queries_lo(0)
                    queries_lo(1)
                else:
                    mix_lo(3)

            def group_rstd(t0, t1, n_squares, n_root, n_rstd, meanwhile):
                c = slice(t0, t1)
                dve.wait_ge(o_sq, n_squares)
                link(nc.vector.tensor_reduce(ssum[:, c], ss4[:, c, :], AX.X, ALU.add))
                nc.vector.tensor_scalar(mean[:, c], ssum[:, c], 1.0 / D, EPS, ALU.mult,
                                        ALU.add).then_inc(mean_done, 1)
                for t in range(t0, t1):
                    meanwhile(t)
                dve.wait_ge(root_done, n_root)
                inverse_root(mean[:, c], root[:, c], y0[:, c], yy[:, c], cc_[:, c],
                             rstd[:, c]).then_inc(rstd_ready, 1)
                dve.wait_ge(rstd_ready, n_rstd)

            mix_lo(0)
            mix_lo(1)
            for i in range(16):
                q = Q_OUT + i
                if i == 3:
                    dve.wait_ge(gpost_in, 16)
                    dve.wait_ge(x_again, 16 * TB)
                if i % 4 == 3:
                    cb = i // 4
                    for t in range(TB):
                        def take(t):
                            nc.vector.tensor_tensor(mixn[:, t, 512 * cb:512 * cb + 512], bank[4 * (cb % 2) + t],
                                                    gpost[:, 512 * cb:512 * cb + 512], ALU.mult
                                                    ).then_inc(o_taken, 1)

                        if cb < 3:
                            dve.wait_ge(o_sq, 4 * cb + t + 1)
                            take(t)
                    for n, (t0, t1) in enumerate(NORM_GROUPS if cb == 3 else ()):
                        group_rstd(t0, t1, 12 + t1, 3 + n + 1, n + 1, take)
                        for t in range(t0, t1):
                            dve.wait_ge(o_taken, O_BASE - TB + t + 1)
                            residual(mixn, t, slice(0, 512)).then_inc(x1_ready, 1)
                if i < 14:
                    split_lo(q + 2, q % 2)
            for t in range(TB):
                residual(mixn, t, slice(512, 1024)).then_inc(x1_ready, 1)

            for c in range(KD):
                if c == 8:
                    dve.wait_ge(lo_ready, Q_FFN + 1)
                    split_lo(Q_FFN + 1, (Q_FFN + 1) % 2)
                scaled_lo(act_lo[:, c, :], chunk_bank(c), gffn[:, c:c + 1], act_hi[:, c, :])
            norm_column(rcol, 2)
            split_lo(Q_FFN + 2, Q_FFN % 2)
            take_norm_row(rrow, 2)

            dve.wait_ge(acc_zero, 1)

            def times_gain(t, cb):
                if t == 0 and cb == 0:
                    dve.wait_ge(raw_in[Q_END % 2], (Q_END - Q_END % 2) * 8 + 16)
                dve.wait_ge(o_sq, 16 + FINISH.index((t, cb)) + 1)
                a = acc[:, t, 512 * cb:512 * cb + 512]
                nc.vector.tensor_tensor(a, a, raw[Q_END % 2][:, 512 * cb:512 * cb + 512],
                                        ALU.mult).then_inc(gained, 1)

            def feed(b, panels=PER_BLOCK):
                for j in range(panels):
                    q = b * PER_BLOCK + (Q_FFN + j)
                    slot = (Q_FFN + j) % 2
                    i = j // 2
                    if j < 8 and j % 2 == 0:
                        dve.wait_ge(used, q + 1)
                        nc.vector.tensor_tensor(sil[:, :], bank[i % 2], rrow[:, :], ALU.mult).then_inc(gated, 1)
                    if j < 8 and j % 2:
                        dve.wait_ge(silu_done, b * 4 + (i + 1))
                        nc.vector.tensor_tensor(sil[:, :], sil[:, :], rrow[:, :], ALU.mult).then_inc(sil_normed, 1)
                        dve.wait_ge(sil_normed, b * 4 + (i + 1))
                        dve.wait_ge(used, q + 1)
                        nc.vector.tensor_tensor(gf[:, :], bank[2 + i % 2], sil[:, :], ALU.mult).then_inc(g_done, 1)
                        dve.wait_ge(g_hi, b * 4 + (i + 1))
                        nc.vector.tensor_tensor(gt[1][:, i, :], gf[:, :], f(gt[0][:, i, :]),
                                                ALU.subtract).then_inc(g_lo, 1)
                    if j >= 8:
                        cb = j - 8
                        for t in range(TB):
                            if t < TB - 1:
                                dve.wait_ge(d_bank, b * 12 + (3 * cb + t + 1))
                            else:
                                dve.wait_ge(used, q + 1)
                            a = acc[:, t, 512 * cb:512 * cb + 512]
                            nc.vector.tensor_tensor(a, a, bank[(4, 0)[cb % 2] + t], ALU.add).then_inc(o_taken, 1)
                    if not isinstance(b, int) or q > Q_FFN:
                        split_lo(q + 2, slot)

            feed(0)
            with dve.Fori(1, BLOCKS - 1) as b:
                feed(b)
            feed(BLOCKS - 1, 8)

            def last_lo(cb):
                q = Q_END - 4 + cb
                dve.wait_ge(hi_ready, q + 1)
                hi, low = last_down(cb)
                nc.vector.tensor_tensor(low, k4(raw[q % 2]), f(hi), ALU.subtract).then_inc(lo_ready, 1)

            last_lo(2)
            for i, (t, cb) in enumerate(FINISH):
                if i == LATE:
                    last_lo(3)
                dve.wait_ge(d_last, i + 1)
                a = acc[:, t, 512 * cb:512 * cb + 512]
                nc.vector.tensor_tensor(a, a, bank[(i + 4) % 8], ALU.add).then_inc(o_taken, 1)
                if t >= 2 and cb:
                    times_gain(t, cb - 1)
                if cb == 3:
                    if t < 2:
                        for n in range(3):
                            times_gain(t, n)
                    group_rstd(t, t + 1, 16 + i + 1, 7 + t + 1, 3 + t + 1, lambda u: times_gain(u, 3))
                    dve.wait_ge(gained, 4 * t + 4)
                    residual(acc, t, slice(shared(t).stop, D)).then_inc(y_ready, 1)

        @block.tensor
        def _(pe):
            pe.wait_ge(made, 7)
            pe.wait_ge(gpre_in, 16)
            nc.tensor.transpose(bank[7][:, 0:KD], gpre_rows[:, :], ident[0:KD, 0:KD]).then_inc(gains_mm, 1)

            def transposed_and_multiplied(src, before, wait_src, w_panel, operand):
                hi, lo = k16(whi[w_panel % 2]), k16(wlo[w_panel % 2])

                def transpose_chunk(c):
                    wait_src(c)
                    if c >= CHUNK_BANKS:
                        pe.wait_ge(act_l, before + c - CHUNK_BANKS + 1)
                    for t in range(TB):
                        last = nc.tensor.transpose(chunk_bank(c)[:, P * t:P * t + P],
                                                   src[:, t, P * c:P * c + P], ident[:, :])
                    last.then_inc(tr, 1)

                for c in range(AHEAD):
                    transpose_chunk(c)
                for k in range(KD):
                    if k + AHEAD < KD:
                        transpose_chunk(k + AHEAD)
                    if k == 0:
                        pe.wait_ge(lo_ready, w_panel + 1)
                    pe.wait_ge(act_l, before + k + 1)
                    last = three(bank[0], (hi[:, k, :], lo[:, k, :]), (operand[0][:, k, :], operand[1][:, k, :]),
                                 k == 0, k == KD - 1)
                last.then_inc(used, 1)

            def norm_row(col, count):
                pe.wait_ge(rcol_ready, count)
                for t in range(TB):
                    last = nc.tensor.transpose(bank[7][:, P * t:P * t + P], col[:, t, :], ident[:, :])
                last.then_inc(rrow_mm, 1)

            def x_ready(c):
                if c % 4 == 0:
                    pe.wait_ge(x_in[c // 4], 16)
            transposed_and_multiplied(xin, 0, x_ready, 0, (act_hi0, act_lo0))
            pe.wait_ge(gain_cols, 1)
            pe.wait_ge(rows_in, 48)
            nc.tensor.transpose(bank[7][:, KD:N_GAIN], gain_rows[:, :],
                                ident[0:N_GAIN - KD, 0:N_GAIN - KD]).then_inc(gains_mm, 1)
            pe.wait_ge(bias_src_in, 32)
            nc.tensor.matmul(bank[6][0:16, 0:BIAS_W], relaug[:, :], bsel[:, :], start=True,
                             stop=True).then_inc(bias_mm, 1)

            def latent_sum(n):
                pe.wait_ge(sq_added, (KL - 1) * (n + 1))
                nc.tensor.matmul(bank[2 + n], ones[:, :], sq_sum[:, :], start=True, stop=True).then_inc(sumsq_c, 1)

            def window(s):
                if s < UNITS:
                    gh, g, n, lo = unit(s)
                    if n == 0:
                        pe.wait_ge(q_lo, 2 * gh + 2)
                    if s == 0:
                        pe.wait_ge(mean_done, 3)
                        pe.wait_ge(act_l, N_SV)
                    if s == 1:
                        pe.wait_ge(taken, N_IN - 2)
                    if s >= 2:
                        pe.wait_ge(s_max, s - 1)
                    keys = slice(P * n - P + lo, P * n + P)
                    for cc in range(2):
                        dst = bank[(s + 1) % 2 * 2 + cc].rearrange("p (e k) -> p e k", e=2)[:, :, lo:256]
                        last = three(dst, [qs[gh % 2][i][:, cc, P * n:P * n + P] for i in range(2)],
                                     [kpad[i][:, g, :, keys] for i in range(2)], True, True)
                    last.then_inc(s_qk, 1)
                if 3 <= s < UNITS + 3:
                    u = s - 3
                    if u == 0:
                        pe.wait_ge(taken, N_IN)
                    pe.wait_ge(s_norm, u + 1)
                    for kb, h in halves(u):
                        if h >= 3:
                            pe.wait_ge(s_lo, h - 2)
                        for cc in range(2):
                            for e in range(2):
                                o = P * (2 * e + cc)
                                last = nc.tensor.transpose(half_bank(h)[:, o:o + P],
                                                           sp[u % 4][:, 2 * cc + e, P * kb:P * kb + P], ident[:, :])
                        last.then_inc(s_t, 1)
                if s >= 4:
                    u = s - 4
                    gh, g, n, lo = unit(u)
                    if u >= 1:
                        pe.wait_ge(s_out, u)
                    parts = [(kb, e, h) for kb, h in halves(u) for e in range(2)]
                    for m, (kb, e, h) in enumerate(parts):
                        pe.wait_ge(s_lo, h + 1)
                        c0 = 64 - 64 * e
                        last = three(bank[7][:, 0:256],
                                     [vpad[i][:, n - 1 + kb, g, c0:c0 + P] for i in range(2)],
                                     [spt[u % 2][i][:, kb, 256 * e:256 * e + 256] for i in range(2)],
                                     m == 0, m == len(parts) - 1)
                    last.then_inc(s_pv, 1)

            for q in range(1, N_IN):
                if q == N_IN - 1:
                    window(0)
                    window(1)
                pe.wait_ge(lo_ready, q + 1)
                if q >= 3:
                    pe.wait_ge(taken, q - 2)
                hi, lo = k16(whi[q % 2]), k16(wlo[q % 2])
                for k in range(KD):
                    last = three(in_bank(q), (hi[:, k, :], lo[:, k, :]), (act_hi0[:, k, :], act_lo0[:, k, :]),
                                 k == 0, k == KD - 1)
                    if q == N_IN - 1 and k in (1, 3):
                        last.then_inc(h_head, 1)
                last.then_inc(used, 1)
                if q == 1:
                    pe.wait_ge(gain_cols, 2)
                    norm_row(rcol0, 1)
                if q in (KL, 2 * KL):
                    latent_sum(q // KL - 1)
                if q == N_IN - 8:
                    pe.wait_ge(taken, N_IN - 8)
                    for t in range(TB):
                        last = nc.tensor.transpose(bank[4][:, P * t:P * t + P], svt[:, P * t:P * t + P], ident[:, :])
                    last.then_inc(sv_t, 1)

            for s in range(2, UNITS + 4):
                window(s)

            def permute(src, n):
                nc.tensor.matmul(bank[7], rot[:, :], src, start=True, stop=True).then_inc(r_perm, 1)

            pe.wait_ge(s_out, UNITS)
            permute(kraw[:, :], 0)

            def rotary_queries(p):
                q = Q_MLA + 2 * p
                pe.wait_ge(lo_ready, q + 1)
                if p:
                    pe.wait_ge(m_max, 4 * (2 * p - 1) + 1)
                hi, lo = k4(whi[q % 2], 384), k4(wlo[q % 2], 384)
                for k in range(KL):
                    r = [w[:, k, 2 * NOPE:384] for w in (hi, lo)]
                    last = three(bank[0], r, (cq[0][:, k, :], cq[1][:, k, :]), k == 0, k == KL - 1)
                last.then_inc(m_proj, 1)

            def queries(p, hh):
                q = Q_MLA + 2 * p
                if p:
                    pe.wait_ge(m_max, 4 * (2 * p - 1) + 2 + hh)
                hi, lo = k4(whi[q % 2], 384), k4(wlo[q % 2], 384)
                for k in range(KL):
                    c0 = NOPE * hh
                    last = three(bank[1 + hh], (hi[:, k, c0:c0 + P], lo[:, k, c0:c0 + P]),
                                 (cq[0][:, k, :], cq[1][:, k, :]), k == 0, k == KL - 1)
                last.then_inc((m_proj, used)[hh], 1)

            def keys_of(p, hh):
                hi, lo = k4(whi[(Q_MLA + 1) % 2]), k4(wlo[(Q_MLA + 1) % 2])
                for k in range(KL):
                    c0 = 256 * hh
                    last = three(bank[hh], (hi[:, k, c0:c0 + P], lo[:, k, c0:c0 + P]),
                                 (ckv[0][:, k, :], ckv[1][:, k, :]), k == 0, k == KL - 1)
                last.then_inc(m_proj, 1)

            def values_of(p, half, b):
                hi, lo = k4(whi[(Q_MLA + 1) % 2]), k4(wlo[(Q_MLA + 1) % 2])
                for t in (2 * half, 2 * half + 1):
                    for k in range(KL):
                        v = [w[:, k, :].rearrange("p (h n) -> p h n", h=2)[:, :, P:256] for w in (hi, lo)]
                        dst = b[:, 256 * (t % 2):256 * (t % 2) + 256]
                        last = three(dst.rearrange("p (h n) -> p h n", h=2),
                                     [ckv[i][:, k, P * t:P * t + P] for i in range(2)], v, k == 0, k == KL - 1)
                last.then_inc((m_proj, used)[half], 1)

            def scores(h):
                p, hh = h // 2, h % 2
                done = N_KR + PER_PAIR * p
                for i in range(TB):
                    if hh:
                        pe.wait_ge(m_max, 4 * (h - 1) + i + 1)
                    elif i < 3:
                        pe.wait_ge(act_l, done + 3 + i)
                    elif h:
                        pe.wait_ge(m_out, h)
                    w = max(256, P * (i + 1))
                    three(bank[i][:, 0:w], [qn[m][:, hh, P * i:P * i + P] for m in range(2)],
                          [kn[m][:, hh, 0:w] for m in range(2)], True, False)
                pe.wait_ge(act_l, done + 7)
                for i in range(TB):
                    w = max(256, P * (i + 1))
                    rows = slice(64 * hh, 64 * hh + 64)
                    nc.tensor.matmul(bank[i][:, 0:w], qr[hh][:, P * i:P * i + P], kr[0][:, 0:w],
                                     start=False, stop=False)
                    nc.tensor.matmul(bank[i][:, 0:w], qr[hh][rows, P * i:P * i + P], kr[1][rows, 0:w],
                                     start=False, stop=True).then_inc(m_qk, 1)

            def transposes(h):
                pe.wait_ge(m_norm, 4 * h + 4)
                for n, blocks in enumerate((((0, 0), (0, 1), (0, 2), (0, 3)), ((1, 1), (1, 2), (1, 3)),
                                            ((2, 2), (2, 3), (3, 2), (3, 3)))):
                    if h:
                        pe.wait_ge(m_lo, 3 * (h - 1) + n + 1)
                    elif n == 0:
                        pe.wait_ge(s_lo, N_HALVES)
                    for o, (j, i) in enumerate(blocks):
                        last = nc.tensor.transpose(bank[4 + n][:, P * o:P * o + P],
                                                   mp[h % 2][:, i, P * j:P * j + P], ident[:, :])
                    last.then_inc(m_t, 1)

            def values(h):
                p, hh = h // 2, h % 2
                if h == MLA_HEADS - 1:
                    pe.wait_ge(m_out, h)
                elif hh:
                    pe.wait_ge(m_max, 4 * h + 4)
                pe.wait_ge(act_l, N_KR + PER_PAIR * (p + 1) + (4 if p == PAIRS - 1 else 0))
                for j, (o, w, n) in enumerate(((0, 512, 1), (512, 384, 2), (896, 256, 3), (1152, 256, 3))):
                    pe.wait_ge(m_lo, 3 * h + n)
                    last = three(value_bank(h)[:, 512 - w:512], [vn[m][:, j, P * hh:P * hh + P] for m in range(2)],
                                 [mpt[h % 2][m][:, o:o + w] for m in range(2)], j == 0, j == TB - 1)
                last.then_inc(m_pv, 1)

            def out_products(i, order):
                q = Q_OUT + i
                cb, kg = i // 4, KG_ORDER[i % 4]
                hi, lo = k4(whi[q % 2]), k4(wlo[q % 2])
                for k, t in order:
                    if i < 4 and t == 0:
                        pe.wait_ge(act_l, N_KG2 - 3 + k if i == 0 else N_PAIRS + 4 * i + k + 1)
                    if i % 4 == 0 and k == 0 and cb >= 2:
                        pe.wait_ge(o_taken, 4 * (cb - 2) + t + 1)
                    last = three(bank[4 * (cb % 2) + t], [mixt[kg][m][:, k, P * t:P * t + P] for m in range(2)],
                                 (hi[:, k, :], lo[:, k, :]), i % 4 == 0 and k == 0, i % 4 == 3 and k == 3)
                    if i % 4 == 3 and k == 3 and t < TB - 1:
                        last.then_inc(o_bank, 1)
                return last

            pe.wait_ge(s_max, UNITS)
            rotary_queries(0)
            queries(0, 0)
            queries(0, 1)
            for p in range(PAIRS):
                pe.wait_ge(lo_ready, Q_MLA + 2 * p + 2)
                pe.wait_ge(r_in, p + 1)
                keys_of(p, 0)
                pe.wait_ge(r_done, p + 1)
                if p:
                    pe.wait_ge(m_out, 2 * p - 1)
                permute(t_sb[:, :], p + 1)
                pe.wait_ge(act_l, N_KR + PER_PAIR * p + 1)
                keys_of(p, 1)
                pe.wait_ge(act_l, N_KR + PER_PAIR * p + 2)
                values_of(p, 0, bank[2])
                scores(2 * p)
                pe.wait_ge(r_done, p + 2)
                values_of(p, 1, bank[7])
                scores(2 * p + 1)
                transposes(2 * p)
                if p < PAIRS - 1:
                    rotary_queries(p + 1)
                else:
                    pe.wait_ge(lo_ready, Q_OUT + 1)
                    pe.wait_ge(m_max, 4 * MLA_HEADS)
                    out_products(0, [(k, t) for k in (0, 1) for t in range(TB)])
                values(2 * p)
                transposes(2 * p + 1)
                if p < PAIRS - 1:
                    queries(p + 1, 0)
                else:
                    out_products(0, [(k, t) for k in (2, 3) for t in range(TB)]).then_inc(used, 1)
                values(2 * p + 1)
                if p < PAIRS - 1:
                    queries(p + 1, 1)

            for i in range(1, 16):
                pe.wait_ge(lo_ready, Q_OUT + i + 1)
                if i == 4:
                    pe.wait_ge(m_lo, 3 * MLA_HEADS)
                    pe.wait_ge(m_out, MLA_HEADS)
                order = [(k, t) for k in range(4) for t in range(TB)]
                if i % 4 == 3:
                    order = [(k, t) for t in range(TB) for k in range(4)]
                out_products(i, order).then_inc(used, 1)

            def x1_chunk_ready(c):
                if c % 4 == 0 and c < 8:
                    pe.wait_ge(x1_ready, TB * (c // 4 + 1))
                if c >= 8 and c % 4 == 0:
                    pe.wait_ge(x1_pool, 2 * TB)
                if c == 0:
                    pe.wait_ge(o_taken, O_BASE)

            transposed_and_multiplied(x1, N_MIX, x1_chunk_ready, Q_FFN, (act_hi, act_lo))

            def feed(b, panels=PER_BLOCK):
                first = isinstance(b, int) and b == 0
                for j in range(1 if first else 0, panels):
                    q = b * PER_BLOCK + (Q_FFN + j)
                    slot = (Q_FFN + j) % 2
                    i = j // 2
                    pe.wait_ge(lo_ready, q + 1)
                    if j < 8:
                        dst = bank[2 * (j % 2) + i % 2]
                        if j < 4 and not first:
                            pe.wait_ge(o_taken, b * 16 + (O_BASE - 3 + (0, 2, 1, 3)[j]))
                        elif j >= 4:
                            pe.wait_ge((gated, g_done)[j % 2], b * 4 + (i - 1))
                        hi, lo = k16(whi[slot]), k16(wlo[slot])
                        for k in range(KD):
                            last = three(dst, (hi[:, k, :], lo[:, k, :]), (act_hi[:, k, :], act_lo[:, k, :]),
                                         k == 0, k == KD - 1)
                    else:
                        d = j - 8
                        hi, lo = k4(whi[slot]), k4(wlo[slot])
                        order = [(k, t) for t in range(TB) for k in range(4)]
                        if d == 0:
                            order = [(k, t) for k in range(4) for t in range(TB)]
                        for k, t in order:
                            if d == 0 and t == 0:
                                pe.wait_ge(g_lo, b * 4 + (k + 1))
                            if d >= 2 and k == 0:
                                pe.wait_ge(o_taken, b * 16 + (O_BASE + 4 * (d - 2) + t + 1))
                            last = three(bank[(4, 0)[d % 2] + t], [gt[m][:, k, P * t:P * t + P] for m in range(2)],
                                         (hi[:, k, :], lo[:, k, :]), k == 0, k == 3)
                            if k == 3 and t < TB - 1:
                                last.then_inc(d_bank, 1)
                    last.then_inc(used, 1)
                    if first and j == 1:
                        norm_row(rcol, 2)

            feed(0)
            with pe.Fori(1, BLOCKS - 1) as b:
                feed(b)
            feed(BLOCKS - 1, 8)
            for i, (t, cb) in enumerate(FINISH):
                hi, lo = last_down(cb)
                if t == 0:
                    pe.wait_ge(lo_ready, Q_END - 4 + cb + 1)
                if i >= 8:
                    pe.wait_ge(o_taken, O_BASE + 16 * (BLOCKS - 1) + i - 7)
                for k in range(4):
                    if i == 0:
                        pe.wait_ge(g_lo, 4 * (BLOCKS - 1) + k + 1)
                    last = three(bank[(i + 4) % 8], [gt[m][:, k, P * t:P * t + P] for m in range(2)],
                                 (hi[:, k, :], lo[:, k, :]), k == 0, k == 3)
                last.then_inc(d_last, 1)


_INS = ["x", "positions", "g_mix_pre", "w_in", "g_cq", "g_ckv", "w_uq", "w_ukv", "sinks", "rel_bias", "w_o",
        "g_mix_post", "g_ffn_pre", "w_gate", "w_up", "w_down", "g_ffn_post"]


def kernel(**inputs):
    import concourse.bacc as bacc
    from concourse.bass_utils import run_bass_kernel_spmd

    nc = bacc.Bacc("TRN2", target_bir_lowering=False, num_devices=1)
    arrays, args = {}, []
    given = [(name, np.ascontiguousarray(inputs[name])) for name in _INS]
    given += [("buckets", bucket_rows()), ("inv_freq", inverse_frequencies())]
    for name, a in given:
        arrays[f"in_{name}"] = a
        args.append(nc.dram_tensor(f"in_{name}", a.shape, mybir.dt.from_np(a.dtype), kind="ExternalInput").ap())
    out = nc.dram_tensor("out_dram", (1, S, D), F32, kind="ExternalOutput").ap()
    build(nc, *args, out)
    r = run_bass_kernel_spmd(nc, [arrays], core_ids=[0])
    return r.results[0]["out_dram"]
```
